# Optimizing a Trainium2 kernel written in Bass

```python
import jax, jax.numpy as jnp
from jax import lax
import numpy as np

D_MODEL = 2048
BATCH = 1
SEQ = 256
DEPTH = 1

POOL_WIDTH = 1024
POOL_GROUPS = 4
POOL_WINDOWS = (2, 4, 8, 16)
POOL_GROUP_DIM = POOL_WIDTH // POOL_GROUPS
CONF_WIDTH = 1024
CONF_KERNEL = 31
SCONV_WIDTH = 1024
SCONV_KERNEL = 3
N_BRANCH = 3
OFF_POOL = POOL_WIDTH
OFF_CONF = OFF_POOL + 2 * CONF_WIDTH
OFF_SCONV = OFF_CONF + 3 * SCONV_WIDTH
D_IN = OFF_SCONV + N_BRANCH * D_MODEL
D_FF = 5504
FFN_KERNEL = 3
EPS = 1e-6


def rms_norm(x, g):
    xf = x.astype(jnp.float32)
    y = xf * lax.rsqrt(jnp.mean(xf * xf, axis=-1, keepdims=True) + EPS)
    return (y * g.astype(jnp.float32)).astype(x.dtype)

def layer_norm(x, g, b):
    xf = x.astype(jnp.float32)
    mu = jnp.mean(xf, axis=-1, keepdims=True)
    xc = xf - mu
    var = jnp.mean(xc * xc, axis=-1, keepdims=True)
    y = xc * lax.rsqrt(var + EPS) * g.astype(jnp.float32) + b.astype(jnp.float32)
    return y.astype(x.dtype)

def causal_dwconv(x, w):
    k, c = w.shape
    return lax.conv_general_dilated(
        x, w[:, None, :].astype(x.dtype), window_strides=(1,), padding=[(k - 1, 0)],
        dimension_numbers=('NWC', 'WIO', 'NWC'), feature_group_count=c)

def multiscale_pool(u, w_grp, scale):
    b, s, _ = u.shape
    ug = u.reshape(b, s, POOL_GROUPS, POOL_GROUP_DIM).astype(jnp.float32)
    cs0 = jnp.pad(jnp.cumsum(ug, axis=1), ((0, 0), (1, 0), (0, 0), (0, 0)))
    pos = jnp.arange(1, s + 1, dtype=jnp.float32)
    outs = []
    for g, w in enumerate(POOL_WINDOWS):
        cg = cs0[:, :, g]
        lagged = jnp.pad(cg[:, :s + 1 - w], ((0, 0), (w, 0), (0, 0)))
        window_sum = cg[:, 1:] - lagged[:, 1:]
        count = jnp.minimum(pos, float(w))[None, :, None]
        outs.append(window_sum / count - ug[:, :, g])
    pooled = jnp.stack(outs, axis=2).astype(u.dtype)
    mixed = jnp.einsum('bsgc,gcd->bsgd', pooled, w_grp)
    return mixed.reshape(b, s, POOL_WIDTH) * scale

def first_inputs(seed: int = 0) -> dict:
    key = jax.random.key(seed)
    ks = jax.random.split(key, 24)
    L, D = DEPTH, D_MODEL
    nrm = lambda k, shape, fan: jax.random.normal(k, shape, jnp.float32) * (fan ** -0.5)
    gain = lambda k, shape: 1.0 + 0.05 * jax.random.normal(k, shape, jnp.float32)
    small = lambda k, shape: 0.02 * jax.random.normal(k, shape, jnp.float32)
    return {
        'x': jax.random.normal(ks[0], (BATCH, SEQ, D), jnp.float32),
        'norm1_g': gain(ks[1], (L, D)),
        'w_in': nrm(ks[2], (L, D, D_IN), D),
        'gate_b': small(ks[3], (L, N_BRANCH * D)),
        'pool_w': nrm(ks[4], (L, POOL_GROUPS, POOL_GROUP_DIM, POOL_GROUP_DIM), POOL_GROUP_DIM),
        'pool_scale': gain(ks[5], (L, POOL_WIDTH)),
        'pool_proj': nrm(ks[6], (L, POOL_WIDTH, D), POOL_WIDTH),
        'conf_conv_w': nrm(ks[7], (L, CONF_KERNEL, CONF_WIDTH), CONF_KERNEL),
        'conf_conv_b': small(ks[8], (L, CONF_WIDTH)),
        'conf_ln_g': gain(ks[9], (L, CONF_WIDTH)),
        'conf_ln_b': small(ks[10], (L, CONF_WIDTH)),
        'conf_proj': nrm(ks[11], (L, CONF_WIDTH, D), CONF_WIDTH),
        'sconv_w': nrm(ks[12], (L, SCONV_KERNEL, SCONV_WIDTH), SCONV_KERNEL),
        'sconv_proj': nrm(ks[13], (L, SCONV_WIDTH, D), SCONV_WIDTH),
        'w_o': nrm(ks[14], (L, D, D), D),
        'norm2_g': gain(ks[15], (L, D)),
        'ffn_up': nrm(ks[16], (L, D, 2 * D_FF), D),
        'ffn_conv_w': nrm(ks[17], (L, FFN_KERNEL, 2 * D_FF), FFN_KERNEL),
        'ffn_down': nrm(ks[18], (L, D_FF, D), D_FF),
        'final_g': gain(ks[19], (D,)),
    }

def first_block(x, norm1_g, w_in, gate_b, pool_w, pool_scale, pool_proj, conf_conv_w, conf_conv_b,
              conf_ln_g, conf_ln_b, conf_proj, sconv_w, sconv_proj, w_o, norm2_g, ffn_up, ffn_conv_w,
              ffn_down, final_g):
    for l in range(DEPTH):
        h = rms_norm(x, norm1_g[l])
        z = h @ w_in[l]
        u_pool, u_conf, u_sc, gate_logits = jnp.split(z, [OFF_POOL, OFF_CONF, OFF_SCONV], axis=-1)
        br_a = multiscale_pool(u_pool, pool_w[l], pool_scale[l]) @ pool_proj[l]
        val, gte = jnp.split(u_conf, 2, axis=-1)
        v = val * jax.nn.sigmoid(gte)
        v = causal_dwconv(v, conf_conv_w[l]) + conf_conv_b[l]
        v = jax.nn.silu(layer_norm(v, conf_ln_g[l], conf_ln_b[l]))
        br_b = v @ conf_proj[l]
        bg, cg, hs = jnp.split(u_sc, 3, axis=-1)
        br_c = (bg * causal_dwconv(cg * hs, sconv_w[l])) @ sconv_proj[l]
        ga, gb, gc = jnp.split(jax.nn.sigmoid(gate_logits + gate_b[l]), 3, axis=-1)
        x = x + (ga * br_a + gb * br_b + gc * br_c) @ w_o[l]
        h = rms_norm(x, norm2_g[l])
        up = causal_dwconv(h @ ffn_up[l], ffn_conv_w[l])
        gt, vl = jnp.split(up, 2, axis=-1)
        x = x + (jax.nn.silu(gt) * vl) @ ffn_down[l]
    return rms_norm(x, final_g)


DEPTH_2 = 2

GRID_W = 64
CTX_LEN = 256

HD = 64
H_A = 8
D_A = H_A * HD
H_B = 12
HKV_B = 4
D_B = H_B * HD
KV_B = HKV_B * HD
H_C = 6
NOPE_C = 128
ROPE_DIM = 64
QK_C = NOPE_C + ROPE_DIM
V_C = 128
D_C = H_C * V_C
Q_LORA = 768
KV_LORA = 512
D_MIX = D_A + D_B + D_C
N_IN = 3 * D_A + D_B + 2 * KV_B + Q_LORA + KV_LORA + ROPE_DIM + D_MIX

NA_ROWS = 8
NA_COLS = 16
SW_WINDOW = 128
SW_BLOCK = 128
Q_BLOCK = 128

ROPE_BASE = 10000.0
ADA_SCALE = 0.5
NEG_INF = -1e30


def rms(x, w):
    xf = x.astype(jnp.float32)
    y = xf * lax.rsqrt(jnp.mean(xf * xf, axis=-1, keepdims=True) + EPS)
    return (y * w.astype(jnp.float32)).astype(x.dtype)

def axial_rope(L, dim, dtype):
    t = jnp.arange(L)
    row = (t // GRID_W).astype(jnp.float32)
    col = (t % GRID_W).astype(jnp.float32)
    n_freq = dim // 4
    inv = ROPE_BASE ** (-jnp.arange(n_freq, dtype=jnp.float32) / n_freq)
    ar = row[:, None] * inv
    ac = col[:, None] * inv
    ang = jnp.concatenate([ar, ar, ac, ac], axis=-1)
    return jnp.cos(ang).astype(dtype), jnp.sin(ang).astype(dtype)

def apply_rope2d(x, cos, sin):
    x1, x2, x3, x4 = jnp.split(x, 4, axis=-1)
    rot = jnp.concatenate([-x2, x1, -x4, x3], axis=-1)
    return x * cos[None, :, None, :] + rot * sin[None, :, None, :]

def split_points():
    sizes = (D_A, D_A, D_A, D_B, KV_B, KV_B, Q_LORA, KV_LORA, ROPE_DIM, D_MIX)
    return [int(p) for p in np.cumsum(sizes)[:-1]]

def project_stream(h, w_in, qn_a, kn_a, qn_b, kn_b, qa_norm, kva_norm, w_qb, w_kvb, qn_c, kn_c, rope):
    B, L, _ = h.shape
    u = h @ w_in
    qa, ka, va, qb, kb, vb, cq, ckv, kpe, z = jnp.split(u, split_points(), axis=-1)

    def heads(t, n):
        return t.reshape(B, L, n, -1)

    qa = rms(heads(qa, H_A), qn_a)
    ka = rms(heads(ka, H_A), kn_a)
    va = heads(va, H_A)
    qb = rms(heads(qb, H_B), qn_b)
    kb = rms(heads(kb, HKV_B), kn_b)
    vb = heads(vb, HKV_B)
    qc = rms(heads(rms(cq, qa_norm) @ w_qb, H_C), qn_c)
    kvc = heads(rms(ckv, kva_norm) @ w_kvb, H_C)
    kc = jnp.concatenate(
        [kvc[..., :NOPE_C], jnp.broadcast_to(kpe[:, :, None, :], (B, L, H_C, ROPE_DIM))], axis=-1)
    kc = rms(kc, kn_c)
    vc = kvc[..., NOPE_C:]
    if rope is not None:
        cos, sin = rope
        qb = apply_rope2d(qb, cos, sin)
        kb = apply_rope2d(kb, cos, sin)
        qc = jnp.concatenate([qc[..., :NOPE_C], apply_rope2d(qc[..., NOPE_C:], cos, sin)], axis=-1)
        kc = jnp.concatenate([kc[..., :NOPE_C], apply_rope2d(kc[..., NOPE_C:], cos, sin)], axis=-1)
    return (qa, ka, va, qb, kb, vb, qc, kc, vc, z)

def natten_latent(q, k, v, kc, vc, rpb):
    B, L, H, D = q.shape
    rows = L // GRID_W
    wr = min(NA_ROWS, rows)
    ncb = GRID_W // NA_COLS
    span = 2 * NA_COLS
    cb = np.arange(ncb)
    kcol = np.clip(cb * NA_COLS - NA_COLS // 2, 0, GRID_W - span)[:, None] + np.arange(span)
    qcol = cb[:, None] * NA_COLS + np.arange(NA_COLS)
    qstart = np.clip(qcol - NA_COLS // 2, 0, GRID_W - NA_COLS)
    col_ok = (kcol[:, None, :] >= qstart[:, :, None]) & (kcol[:, None, :] < qstart[:, :, None] + NA_COLS)
    dc_idx = (np.clip(kcol[:, None, :] - qcol[:, :, None], -(NA_COLS - 1), NA_COLS - 1)
              + NA_COLS - 1).astype(np.int32)
    qg = q.reshape(B, rows, ncb, NA_COLS, H, D)
    kg = k.reshape(B, rows, GRID_W, H, D)[:, :, kcol]
    vg = v.reshape(B, rows, GRID_W, H, D)[:, :, kcol]
    scale = D ** -0.5
    n_loc = wr * span

    def row_fn(r):
        rs = jnp.clip(r - wr // 2, 0, rows - wr)
        qr = lax.dynamic_index_in_dim(qg, r, axis=1, keepdims=False)
        kr = lax.dynamic_slice_in_dim(kg, rs, wr, axis=1)
        vr = lax.dynamic_slice_in_dim(vg, rs, wr, axis=1)
        dr_idx = rs + jnp.arange(wr) - r + NA_ROWS - 1
        bias = rpb[:, dr_idx[None, None, :, None], dc_idx[:, :, None, :]]
        s_loc = jnp.einsum('bnqhd,brnkhd->bhnqrk', qr, kr,
                           preferred_element_type=jnp.float32) * scale + bias
        s_loc = jnp.where(col_ok[:, :, None, :], s_loc, NEG_INF)
        s_ctx = jnp.einsum('bnqhd,bchd->bhnqc', qr, kc, preferred_element_type=jnp.float32) * scale
        s = jnp.concatenate([s_loc.reshape(B, H, ncb, NA_COLS, n_loc), s_ctx], axis=-1)
        p = jax.nn.softmax(s, axis=-1).astype(v.dtype)
        p_loc = p[..., :n_loc].reshape(B, H, ncb, NA_COLS, wr, span)
        o = (jnp.einsum('bhnqrk,brnkhd->bnqhd', p_loc, vr)
             + jnp.einsum('bhnqc,bchd->bnqhd', p[..., n_loc:], vc))
        return o.reshape(B, GRID_W, H, D)

    o = lax.map(row_fn, jnp.arange(rows))
    return o.transpose(1, 0, 2, 3, 4).reshape(B, L, H, D)

def swa_latent(q, k, v, kc, vc, sink):
    B, L, H, D = q.shape
    Hkv = k.shape[2]
    G = H // Hkv
    Lc = kc.shape[1]
    nb = L // SW_BLOCK
    span = SW_BLOCK + 2 * SW_WINDOW
    pad = ((0, 0), (SW_WINDOW, SW_WINDOW), (0, 0), (0, 0))
    kp = jnp.pad(k, pad)
    vp = jnp.pad(v, pad)
    qb = q.reshape(B, nb, SW_BLOCK, Hkv, G, D).transpose(1, 0, 2, 3, 4, 5)
    snk = sink.reshape(Hkv, G).astype(jnp.float32)[None, :, :, None, None]
    scale = D ** -0.5

    def blk(args):
        i, qi = args
        k0 = i * SW_BLOCK
        ki = lax.dynamic_slice_in_dim(kp, k0, span, axis=1)
        vi = lax.dynamic_slice_in_dim(vp, k0, span, axis=1)
        qpos = k0 + jnp.arange(SW_BLOCK)
        kpos = k0 - SW_WINDOW + jnp.arange(span)
        ok = (kpos >= 0) & (kpos < L) & (jnp.abs(qpos[:, None] - kpos[None, :]) <= SW_WINDOW)
        s_loc = jnp.einsum('bqkgd,bjkd->bkgqj', qi, ki, preferred_element_type=jnp.float32) * scale
        s_loc = jnp.where(ok, s_loc, NEG_INF)
        s_ctx = jnp.einsum('bqkgd,bckd->bkgqc', qi, kc, preferred_element_type=jnp.float32) * scale
        s = jnp.concatenate([s_loc, s_ctx, jnp.broadcast_to(snk, s_loc.shape[:-1] + (1,))], axis=-1)
        p = jax.nn.softmax(s, axis=-1).astype(v.dtype)
        o = (jnp.einsum('bkgqj,bjkd->bqkgd', p[..., :span], vi)
             + jnp.einsum('bkgqc,bckd->bqkgd', p[..., span:span + Lc], vc))
        return o.reshape(B, SW_BLOCK, H, D)

    o = lax.map(blk, (jnp.arange(nb), qb))
    return o.transpose(1, 0, 2, 3, 4).reshape(B, L, H, D)

def mla_latent(q, k, v, kc, vc):
    B, L, H, D = q.shape
    Dv = v.shape[-1]
    nb = L // Q_BLOCK
    k_all = jnp.concatenate([kc, k], axis=1)
    v_all = jnp.concatenate([vc, v], axis=1)
    qb = q.reshape(B, nb, Q_BLOCK, H, D).transpose(1, 0, 2, 3, 4)
    scale = D ** -0.5

    def blk(qi):
        s = jnp.einsum('bqhd,bkhd->bhqk', qi, k_all, preferred_element_type=jnp.float32) * scale
        p = jax.nn.softmax(s, axis=-1).astype(v.dtype)
        return jnp.einsum('bhqk,bkhd->bqhd', p, v_all)

    o = lax.map(blk, qb)
    return o.transpose(1, 0, 2, 3, 4).reshape(B, L, H, Dv)

def ctx_attn(q, k, v, sink=None):
    B, Lc, H, D = q.shape
    Hkv = k.shape[2]
    G = H // Hkv
    qg = q.reshape(B, Lc, Hkv, G, D)
    s = jnp.einsum('bqkgd,bckd->bkgqc', qg, k, preferred_element_type=jnp.float32) * (D ** -0.5)
    if sink is not None:
        snk = sink.reshape(Hkv, G).astype(jnp.float32)[None, :, :, None, None]
        s = jnp.concatenate([s, jnp.broadcast_to(snk, s.shape[:-1] + (1,))], axis=-1)
    p = jax.nn.softmax(s, axis=-1)[..., :Lc].astype(v.dtype)
    return jnp.einsum('bkgqc,bckd->bqkgd', p, v).reshape(B, Lc, H, v.shape[-1])

def merge_out(o_a, o_b, o_c, z, w_out):
    B, L = o_a.shape[:2]
    y = jnp.concatenate([o_a.reshape(B, L, -1), o_b.reshape(B, L, -1), o_c.reshape(B, L, -1)], axis=-1)
    return (y * jax.nn.silu(z)) @ w_out

def second_inputs(seed: int = 0) -> dict:
    key = jax.random.key(seed)
    ks = jax.random.split(key, 21)
    f32 = jnp.float32

    def nrm(k, shape, s):
        return jax.random.normal(k, shape, f32) * s

    def gain(k, shape):
        return 1.0 + 0.02 * jax.random.normal(k, shape, f32)

    return {
        "x": nrm(ks[0], (BATCH, SEQ, D_MODEL), 1.0),
        "c": nrm(ks[1], (BATCH, D_MODEL), 1.0),
        "ctx": nrm(ks[2], (BATCH, CTX_LEN, D_MODEL), 1.0),
        "c_ctx": nrm(ks[3], (D_MODEL,), 1.0),
        "norm_w": gain(ks[4], (DEPTH_2, D_MODEL)),
        "w_ada": nrm(ks[5], (DEPTH_2, D_MODEL, 3 * D_MODEL), ADA_SCALE * D_MODEL ** -0.5),
        "b_ada": nrm(ks[6], (DEPTH_2, 3 * D_MODEL), 0.01),
        "w_in": nrm(ks[7], (DEPTH_2, D_MODEL, N_IN), D_MODEL ** -0.5),
        "qn_a": gain(ks[8], (DEPTH_2, HD)),
        "kn_a": gain(ks[9], (DEPTH_2, HD)),
        "rpb_a": nrm(ks[10], (DEPTH_2, H_A, 2 * NA_ROWS - 1, 2 * NA_COLS - 1), 0.1),
        "qn_b": gain(ks[11], (DEPTH_2, HD)),
        "kn_b": gain(ks[12], (DEPTH_2, HD)),
        "sink_b": nrm(ks[13], (DEPTH_2, H_B), 0.5),
        "qa_norm": gain(ks[14], (DEPTH_2, Q_LORA)),
        "kva_norm": gain(ks[15], (DEPTH_2, KV_LORA)),
        "w_qb": nrm(ks[16], (DEPTH_2, Q_LORA, H_C * QK_C), Q_LORA ** -0.5),
        "w_kvb": nrm(ks[17], (DEPTH_2, KV_LORA, H_C * (NOPE_C + V_C)), KV_LORA ** -0.5),
        "qn_c": gain(ks[18], (DEPTH_2, QK_C)),
        "kn_c": gain(ks[19], (DEPTH_2, QK_C)),
        "w_out": nrm(ks[20], (DEPTH_2, D_MIX, D_MODEL), D_MIX ** -0.5),
    }

def second_block(x, c, ctx, c_ctx, norm_w, w_ada, b_ada, w_in, qn_a, kn_a, rpb_a, qn_b, kn_b, sink_b,
              qa_norm, kva_norm, w_qb, w_kvb, qn_c, kn_c, w_out):
    B, L, _ = x.shape
    cos, sin = axial_rope(L, ROPE_DIM, x.dtype)
    sc = jax.nn.silu(c)
    scc = jax.nn.silu(c_ctx)
    xc = ctx
    for l in range(DEPTH_2):
        last = l == DEPTH_2 - 1
        shift, scale, gate = jnp.split(sc @ w_ada[l] + b_ada[l], 3, axis=-1)
        shift_c, scale_c, gate_c = jnp.split(scc @ w_ada[l] + b_ada[l], 3, axis=-1)
        h = rms(x, norm_w[l]) * (1.0 + scale[:, None]) + shift[:, None]
        hc = rms(xc, norm_w[l]) * (1.0 + scale_c) + shift_c
        weights = (w_in[l], qn_a[l], kn_a[l], qn_b[l], kn_b[l], qa_norm[l], kva_norm[l],
                   w_qb[l], w_kvb[l], qn_c[l], kn_c[l])
        qa, ka, va, qb, kb, vb, qc, kc, vc, z = project_stream(h, *weights, rope=(cos, sin))
        qa_c, ka_c, va_c, qb_c, kb_c, vb_c, qc_c, kc_c, vc_c, z_c = project_stream(hc, *weights, rope=None)
        o_a = natten_latent(qa, ka, va, ka_c, va_c, rpb_a[l])
        o_b = swa_latent(qb, kb, vb, kb_c, vb_c, sink_b[l])
        o_c = mla_latent(qc, kc, vc, kc_c, vc_c)
        x = x + gate[:, None] * merge_out(o_a, o_b, o_c, z, w_out[l])
        if not last:
            oa_c = ctx_attn(qa_c, ka_c, va_c)
            ob_c = ctx_attn(qb_c, kb_c, vb_c, sink_b[l])
            oc_c = ctx_attn(qc_c, kc_c, vc_c)
            xc = xc + gate_c * merge_out(oa_c, ob_c, oc_c, z_c, w_out[l])
    return x


def setup_inputs(seed=0):
    out = dict(first_inputs(seed))
    for name, value in second_inputs(seed + 1).items():
        if name != "x":
            out[name + "_2"] = value
    return out


def reference(
    x, norm1_g, w_in, gate_b, pool_w, pool_scale, pool_proj, conf_conv_w, conf_conv_b,
    conf_ln_g, conf_ln_b, conf_proj, sconv_w, sconv_proj, w_o, norm2_g, ffn_up, ffn_conv_w,
    ffn_down, final_g, c_2, ctx_2, c_ctx_2, norm_w_2, w_ada_2, b_ada_2, w_in_2, qn_a_2, kn_a_2,
    rpb_a_2, qn_b_2, kn_b_2, sink_b_2, qa_norm_2, kva_norm_2, w_qb_2, w_kvb_2, qn_c_2, kn_c_2,
    w_out_2,
):
    x = first_block(
        x, norm1_g, w_in, gate_b, pool_w, pool_scale, pool_proj, conf_conv_w, conf_conv_b,
        conf_ln_g, conf_ln_b, conf_proj, sconv_w, sconv_proj, w_o, norm2_g, ffn_up, ffn_conv_w,
        ffn_down, final_g,
    )
    return second_block(
        x, c_2, ctx_2, c_ctx_2, norm_w_2, w_ada_2, b_ada_2, w_in_2, qn_a_2, kn_a_2, rpb_a_2,
        qn_b_2, kn_b_2, sink_b_2, qa_norm_2, kva_norm_2, w_qb_2, w_kvb_2, qn_c_2, kn_c_2,
        w_out_2,
    )


_drawn_inputs = setup_inputs


def setup_inputs(seed=0):
    import zlib

    import numpy as np

    out = dict(_drawn_inputs(seed))
    spreads = {}
    factors = {'gate_b': 8.0,
     'pool_scale': 2.673,
     'conf_conv_b': 4.894,
     'conf_ln_g': 3.374,
     'conf_ln_b': 8.0,
     'ctx_2': 3.242,
     'norm_w_2': 8.0,
     'b_ada_2': 8.0,
     'qn_a_2': 8.0,
     'kn_a_2': 8.0,
     'rpb_a_2': 8.0,
     'qn_b_2': 8.0,
     'kn_b_2': 8.0,
     'sink_b_2': 8.0,
     'qa_norm_2': 8.0,
     'kva_norm_2': 8.0,
     'w_qb_2': 4.386,
     'qn_c_2': 8.0,
     'kn_c_2': 8.0}
    for name, (base, spread) in spreads.items():
        noise = np.random.default_rng([zlib.crc32(name.encode()), seed]).standard_normal(out[name].shape)
        drawn = base * np.exp(spread * noise) if base else spread * noise
        out[name] = __import__('jax').numpy.asarray(drawn.astype(out[name].dtype))
    for name, factor in factors.items():
        out[name] = (out[name] * factor).astype(out[name].dtype)
    return out
```

```python
from contextlib import ExitStack

import numpy as np

import concourse.bass as bass
from concourse import mybir

F32 = mybir.dt.float32
F32R = mybir.dt.float32r
ALU = mybir.AluOpType
ACT = mybir.ActivationFunctionType
AX_X = mybir.AxisListType.X

P = 128
D = 2048
S = 256
KD = D // P
EPS = 1e-6
SLOTS = 8
HI_SLOTS = 4
QW = 8 * P
BANKS = 4
T_BANK, O_BANK = (6, 2), (7, 3)
AHEAD = 3

BR = 1024
KB = BR // P
POOL_CONV = 6
POOL_WINDOWS = (2, 4, 8, 16)
PADW = 16
CONF_K = 31
SCONV_K = 3
D_FF = 5504
FF_CH = D_FF // P
FF_GROUP = 8
FF_GROUPS = FF_CH // FF_GROUP
FF_REST = FF_CH - FF_GROUPS * FF_GROUP
FF_K = 3

LAYERS = 2
HD = 64
H_A, H_B, HKV_B, H_C = 8, 12, 4, 6
QK_C = 192
NOPE = 128
Q_LORA, KV_LORA = 768, 512
SW_WINDOW = 128
GRID_W = 64
NA_ROWS, NA_COLS = 8, 16
NEG = -1e30

B_ORDER = [3 * (2 * t + a) + i for t in range(2) for i in range(3) for a in range(2)]

PHASES = [("conf", 32, 16), ("sconv", 48, 24), ("pool", 16, 8), ("mix", 2, 8),
          ("br_c", 48, 32), ("br_a", 48, 32), ("br_b", 48, 32), ("wo", 32, 16),
          ("ffn", 48 * FF_GROUPS, 32 * FF_GROUPS), ("ffn_rest", 4 * FF_REST + 16, 2 * FF_REST + 16),
          ("ada", 96 * LAYERS, 0)]
for _l in range(LAYERS):
    PHASES += [(f"z{_l}", 32, 16), (f"a{_l}", 24, 12), (f"b{_l}", 20, 10), (f"c{_l}", 22, 11),
               (f"qb{_l}", 9, 9), (f"kvb{_l}", 12, 12), (f"out{_l}", 32, 16)]
Q0, T0 = {}, {}
_q = _t = 0
for _name, _nq, _nt in PHASES:
    Q0[_name], T0[_name] = _q, _t
    _q, _t = _q + _nq, _t + _nt
NQ = _q

PARAMS = [("norm1_g", KD), ("norm2_g", KD), ("final_g", KD), ("gate_b", 3 * KD), ("pool_scale", KB),
          ("conf_w", KB * CONF_K), ("conf_b", KB), ("ln_g", KB), ("ln_b", KB), ("sconv_w", KB * SCONV_K),
          ("ffn_w", FF_CH * 2 * FF_K), ("norm_w", LAYERS * KD), ("b_ada", LAYERS * 3 * KD), ("cvec", KD * 2),
          ("qn_a", LAYERS), ("kn_a", LAYERS), ("qn_b", LAYERS), ("kn_b", LAYERS),
          ("qa_norm", LAYERS * 6), ("kva_norm", LAYERS * 4), ("qn_cn", LAYERS), ("qn_cr", LAYERS),
          ("kn_cn", LAYERS), ("kn_cr", LAYERS), ("sink", LAYERS * H_B)]
PO = {}
_o = 0
for _name, _n in PARAMS:
    PO[_name] = _o
    _o += _n
NPARAM = _o
CONSTS = [("ident", P), ("ones", P), ("halves", P), ("rot", P), ("cos", S), ("sin", S), ("swa", 2 * S), ("fold", 2), ("invcount", 4 * PADW)]
CO = {}
_o = 0
for _name, _n in CONSTS:
    CO[_name] = _o
    _o += _n
NCONST = _o

STAGES = ["centered", "third_cat", "acc_cat", "x_wo", "x_ffn", "silu_c"]
for _l in range(LAYERS):
    STAGES += [f"{_s}{_l}" for _s in ("gains", "z", "a", "an", "b", "bn", "br", "c", "qb", "kvb", "qcn", "qcr",
                                      "kpe", "krope", "kcn", "y", "ycat", "out")]
STAGE = {name: n + 1 for n, name in enumerate(STAGES)}


def repeat(eng, count, body, peel=0):
    n = count - peel
    if n > 1:
        with eng.Fori(0, n) as i:
            body(i)
    elif n == 1:
        body(0)
    for i in range(n, count):
        body(i)


def pick(t, j, a, b):
    if isinstance(j, int):
        return t[:, j, a:b]
    return t[:, bass.ds(j, 1), a:b].rearrange("p o c -> p (o c)")


def build(nc, stream, xT, ctxT, params, consts, natten, out):
    resid = nc.dram_tensor("resid_dram", (P, KD * 2 * S), F32, kind="Internal").ap()

    KIB = 1024
    at = {}
    top = [(nc.sbuf_base + 31) // 32 * 32]

    def region(name, size):
        at[name] = top[0]
        top[0] += (size + 31) // 32 * 32
        assert top[0] <= nc.sbuf_usable_end, (name, top[0], nc.sbuf_usable_end)

    def sb(name, shape, dt, where, off=0):
        return nc.alloc_sbuf_tensor_at(name, [P] + list(shape), dt, offset=at[where] + off)

    region("raw", SLOTS * QW * 4)
    region("whi", HI_SLOTS * QW * 4)
    region("x", KD * 2 * S * 4)
    region("hcat", KD * 4 * S * 4)
    region("q", 36 * KIB)
    region("params", NPARAM * 4)
    region("consts", NCONST * 4)
    region("small", (96 * 2 + KD * 10 + 16) * 4)
    region("work", 5 * 520 * 4 + 2 * 512 * 4 + 2 * 256 * 4)
    raw = sb("raw", [SLOTS, QW], F32, "raw")
    wlo = sb("wlo", [SLOTS, QW], F32R, "raw")
    whi = sb("whi", [HI_SLOTS, QW], F32R, "whi")
    X = sb("X", [KD, 2 * S], F32, "x")
    hcat = sb("hcat", [KD, 4 * S], F32R, "hcat")
    thirdcat = sb("thirdcat", [KB, 2 * S], F32R, "q")
    glu = sb("glu", [KB, S], F32, "q", 16 * KIB)
    conv = sb("conv", [KB, S], F32, "q", 24 * KIB)
    qkv = sb("qkv", [12, 2 * S], F32, "q")
    vtok = sb("vtok", [4, 6 * P], F32, "q", 24 * KIB)
    cqk = sb("cqk", [24, 2 * S], F32, "hcat")
    par = sb("par", [NPARAM], F32, "params")
    con = sb("con", [NCONST], F32, "consts")
    o = 0
    ada_t = sb("ada_t", [2, 96], F32, "small", o); o += 96 * 2 * 4
    gain = sb("gain", [KD, 2], F32, "small", o); o += KD * 2 * 4
    ccat = sb("ccat", [KD, 4], F32R, "small", o); o += KD * 4 * 4
    cs = sb("cs", [KD, 2], F32, "small", o); o += KD * 2 * 4
    csig = sb("csig", [KD, 2], F32, "small", o); o += KD * 2 * 4
    stat = sb("stat", [16], F32, "small", o)
    o = 0
    sq = sb("sq", [4, 2 * S], F32, "work", 0)
    rst = sb("rst", [2, 2 * S], F32, "work", 8 * KIB)
    tmp = sb("tmp", [2, 2 * S], F32, "work", 12 * KIB)
    arow = sb("arow", [2, 512], F32, "work", 0)
    sig = sb("sig", [2, S], F32, "work", 0)
    half = sb("half", [4, S], F32, "work", 2 * KIB)
    tap = sb("tap", [2, S], F32, "q", 32 * KIB)
    upad = sb("upad", [5, PADW + S], F32, "work", 6 * KIB)
    SW = 520
    probs = sb("probs", [3, SW], F32, "work", 0)
    scores = sb("scores", [2, SW], F32, "work", 3 * SW * 4)
    probsT = sb("probsT", [2, 4 * P], F32, "work", 5 * SW * 4)
    bias = sb("bias", [2, S], F32, "work", 5 * SW * 4 + 4 * KIB)

    def pv(name, i, n=1):
        if isinstance(i, int):
            return par[:, PO[name] + i:PO[name] + i + n]
        return par[:, bass.ds(i + PO[name], n)]

    def cv(name, a=0, b=None):
        n = dict(CONSTS)[name]
        return con[:, CO[name] + a:CO[name] + (n if b is None else b)]

    with ExitStack() as ctx:
        psum = ctx.enter_context(nc.psum_tensor("psum", [P, 8, 512], F32))

        def sem(name):
            return ctx.enter_context(nc.semaphore(name))

        raw_in = [sem(f"raw_in{i}") for i in range(SLOTS)]
        hi_ready = sem("hi_ready")
        lo_ready = sem("lo_ready")
        weights_used = sem("weights_used")
        psum_free = sem("psum_free")
        params_in = sem("params_in")
        x_in = sem("x_in")
        ctx_in = sem("ctx_in")
        vector_stage = sem("vector_stage")
        sq_ready = sem("sq_ready")
        sq_used = sem("sq_used")
        stat_ready = sem("stat_ready")
        sqrt_ready = sem("sqrt_ready")
        cat_tmp = sem("cat_tmp")
        cat_hi = sem("cat_hi")
        cat_lo = sem("cat_lo")
        sig_ready = sem("sig_ready")
        sig_used = sem("sig_used")
        gate_ready = sem("gate_ready")
        piece_ready = sem("piece_ready")
        piece_hi = sem("piece_hi")
        piece_lo = sem("piece_lo")
        conv_pool = sem("conv_pool")
        conv_ready = sem("conv_ready")
        mean_ready = sem("mean_ready")
        ln_ready = sem("ln_ready")
        ln_act = sem("ln_act")
        acc_hi = sem("acc_hi")
        c_sig = sem("c_sig")
        c_silu = sem("c_silu")
        rows_ready = sem("rows_ready")
        fold_ready = sem("fold_ready")
        rot_ready = sem("rot_ready")
        rot_used = sem("rot_used")
        vt_ready = sem("vt_ready")
        vt_used = sem("vt_used")
        s_ready = sem("s_ready")
        max_ready = sem("max_ready")
        exp_ready = sem("exp_ready")
        rsum_ready = sem("rsum_ready")
        probs_ready = sem("probs_ready")
        t_ready = sem("t_ready")
        pt_ready = sem("pt_ready")
        o_ready = sem("o_ready")
        o_used = sem("o_used")
        bias_in = [sem(f"bias_in{i}") for i in range(2)]
        spilled = sem("spilled")
        resid_in = sem("resid_in")
        out_done = sem("out_done")

        ones = cv("ones")
        halves = cv("halves")
        jobs = []
        src_no = cat_no = 0

        def job(name, srcs, n, width, scale=(), cat=(), after=None, done=None, loff=2 * S):
            nonlocal src_no, cat_no
            jobs.append(dict(name=name, srcs=srcs, n=n, width=width, scale=scale, cat=cat, after=after,
                             done=done, no=len(jobs), src0=src_no, cat0=cat_no, loff=loff))
            src_no += len(srcs)
            cat_no += len(cat)

        def whole(ap):
            return (ap, ones, 0, P)

        def xjob(name, gname, goff, after, cat):
            srcs = [whole(X[:, k, 0:S]) for k in range(KD)]
            if cat:
                pieces = [(X[:, k, 0:S], [(0, S, pv(gname, goff + k), None)], hcat, k) for k in range(KD)]
                job(name, srcs, D, S, cat=pieces, after=after)
            else:
                job(name, srcs, D, S, scale=[(X[:, k, 0:S], pv(gname, goff + k), 0, P) for k in range(KD)],
                    after=after)

        JOBS_OF = {}

        def group(name, fill):
            a = len(jobs)
            fill()
            JOBS_OF[name] = range(a, len(jobs))

        group("norm1", lambda: xjob("norm1", "norm1_g", 0, None, True))
        group("ln", lambda: job("ln", [whole(conv[:, k, :]) for k in range(KB)], BR, S, after="centered"))
        group("norm2", lambda: xjob("norm2", "norm2_g", 0, "x_wo", True))
        group("final", lambda: xjob("final", "final_g", 0, "x_ffn", False))

        def chunks_w(l):
            return 2 * S if l == 0 else S

        QROPE, KN, KR, VC = 6, 9, 15, 18

        def layer_jobs(l):
            def hnorm():
                srcs = [whole(X[:, k, :]) for k in range(KD)]
                pieces = [(X[:, k, :], [(0, S, gain[:, k, 0:1], ada_t[:, 0, 48 * l + k:48 * l + k + 1]),
                                        (S, 2 * S, gain[:, k, 1:2], ada_t[:, 1, 48 * l + k:48 * l + k + 1])], hcat, k)
                          for k in range(KD)]
                job(f"h{l}", srcs, D, 2 * S, cat=pieces, after=f"gains{l}")
            group(f"h{l}", hnorm)

            def heads(base, count, pname, width, after):
                for k in range(count):
                    ap = qkv[:, base + k, 0:width]
                    job(pname, [(ap, halves, 0, P)], HD, width, scale=[(ap, pv(pname, l), 0, P)], after=after)

            def ga():
                heads(0, 4, "qn_a", chunks_w(l), f"a{l}")
                heads(4, 4, "kn_a", 2 * S, f"a{l}")
            group(f"a{l}", ga)

            def gb():
                heads(0, 6, "qn_b", chunks_w(l), f"b{l}")
                heads(6, 2, "kn_b", 2 * S, f"b{l}")
            group(f"b{l}", gb)

            def lora(name, base, count, pname, first):
                w = chunks_w(l) if name == "cq" else 2 * S
                srcs = [whole(qkv[:, base + k, 0:w]) for k in range(count)]
                pieces = [(qkv[:, base + k, 0:w], [(0, w, pv(pname, count * l + k), None)], hcat, first + k)
                          for k in range(count)]
                job(name, srcs, P * count, w, cat=pieces, after=f"c{l}")
            group(f"cq{l}", lambda: lora("cq", 0, 6, "qa_norm", 10))
            group(f"ckv{l}", lambda: lora("ckv", 6, 4, "kva_norm", 12))

            def gq():
                w = chunks_w(l)
                for h in range(H_C):
                    a = HD * (h % 2)
                    rope = cqk[a:a + HD, QROPE + h // 2, 0:w]
                    job("qc", [whole(cqk[:, h, 0:w]), (rope, ones, a, a + HD)], QK_C, w,
                        scale=[(cqk[:, h, 0:w], pv("qn_cn", l), 0, P),
                               (rope, pv("qn_cr", l)[a:a + HD], a, a + HD)], after=f"qb{l}")
            group(f"qc{l}", gq)

            def gk():
                for h in range(H_C):
                    a = HD * (h % 2)
                    job("kc", [whole(cqk[:, KN + h, :]), (qkv[a:a + HD, 10, :], ones, a, a + HD)], QK_C, 2 * S,
                        scale=[(cqk[:, KN + h, :], pv("kn_cn", l), 0, P),
                               (cqk[a:a + HD, KR + h // 2, :], None, a, a + HD)], after=f"krope{l}")
            group(f"kc{l}", gk)

        for l in range(LAYERS):
            layer_jobs(l)

        ropes, ROPES_OF = [], {}
        for l in range(LAYERS):
            for name, targets in ((f"b{l}", [qkv[:, k, 0:S] for k in range(8)]),
                                  (f"qc{l}", [cqk[:, QROPE + t, 0:S] for t in range(3)]),
                                  (f"kpe{l}", [cqk[:, KR, 0:S]])):
                ROPES_OF[name] = range(len(ropes), len(ropes) + len(targets))
                ropes += targets
        vts, VTS_OF = [], {}
        for l in range(LAYERS):
            for name, src, base, count in ((f"a{l}", qkv, 8, 4), (f"b{l}", qkv, 8, 2), (f"c{l}", cqk, VC, 6)):
                VTS_OF[name] = range(len(vts), len(vts) + count)
                vts += [(src[:, base + k, :], k * P) for k in range(count)]

        units, UNITS_OF = [], {}
        biases = []

        def unit(l, kind, h, qt):
            q0 = P * qt
            ctx_q = qt >= 2
            k0, nk = (S, S) if ctx_q else (0, 2 * S)
            u = dict(no=len(units), kind=kind, nk=nk, k0=k0, q0=q0, bias=None, sink=None)
            if kind == "a":
                a, c = HD * (h % 2), h // 2
                u.update(qk=[(qkv[a:a + HD, c, q0:q0 + P], qkv[a:a + HD, 4 + c, k0:k0 + nk])],
                         v=P * c + a, nv=HD, p0=a, y=c, scale=HD ** -0.5)
                if not ctx_q:
                    u["bias"] = len(biases)
                    biases.append((l, h, qt))
            elif kind == "b":
                c, a = h // 2, HD * (h % 2)
                t = c // 3
                u.update(qk=[(qkv[a:a + HD, c, q0:q0 + P], qkv[a:a + HD, 6 + t, k0:k0 + nk])],
                         v=P * t + a, nv=HD, p0=a, y=4 + c, scale=HD ** -0.5,
                         sink=pv("sink", H_B * l + B_ORDER[h]))
                if not ctx_q:
                    u["swa"] = qt
            else:
                a = HD * (h % 2)
                u.update(qk=[(cqk[:, h, q0:q0 + P], cqk[:, KN + h, k0:k0 + nk]),
                             (cqk[a:a + HD, QROPE + h // 2, q0:q0 + P], cqk[a:a + HD, KR + h // 2, k0:k0 + nk])],
                         v=P * h, nv=P, p0=0, y=10 + h, scale=QK_C ** -0.5)
            units.append(u)

        for l in range(LAYERS):
            for kind, heads_ in (("a", H_A), ("b", H_B), ("c", H_C)):
                start = len(units)
                for h in range(heads_):
                    for qt in range(4 if l == 0 else 2):
                        unit(l, kind, h, qt)
                UNITS_OF[f"{kind}{l}"] = range(start, len(units))

        PIECE = {"sconv": 0, "pooled": 8, "mixed": 16, "acc": 24, "ffn": 40}
        N_PIECES = 40 + FF_CH
        SIG = {"conf": 0, "sconv": 8, "br_c": 16, "br_a": 32, "br_b": 48, "ffn": 64, "z0": 64 + FF_CH, "z1": 80 + FF_CH}

        block = ctx.enter_context(nc.Block())

        @block.sync
        def _(sp):
            sp.dma_start(par[:, :], params).then_inc(params_in, 16)
            sp.dma_start(X[:, :, 0:S], xT).then_inc(x_in, 16)
            sp.dma_start(con[:, :], consts).then_inc(params_in, 16)

            def load(i):
                for k in range(SLOTS):
                    n = SLOTS * i + k
                    sp.wait_ge(weights_used, n + 1)
                    src = stream[n] if isinstance(n, int) else \
                        stream[bass.ds(n, 1)].rearrange("a p c -> p (a c)")
                    sp.dma_start(raw[:, k, :], src).then_inc(raw_in[k], 16)

            repeat(sp, NQ // SLOTS, load)
            for n in range(NQ // SLOTS * SLOTS, NQ):
                sp.wait_ge(weights_used, n + 1)
                sp.dma_start(raw[:, n % SLOTS, :], stream[n]).then_inc(raw_in[n % SLOTS], 16)

        @block.scalar
        def _(act):
            def hi(s, d=0):
                if isinstance(d, int) and s + d >= NQ:
                    return
                slot = s % SLOTS
                act.wait_ge(raw_in[slot], 16 * (s // SLOTS + 1) + 16 // SLOTS * d)
                act.wait_ge(weights_used, s + d + SLOTS - HI_SLOTS + 1)
                act.activation(whi[:, s % HI_SLOTS, :], raw[:, slot, :], ACT.Copy).then_inc(hi_ready, 1)

            def plain(name, nq, step, peel=0):
                def body(i):
                    for k in range(step):
                        hi(Q0[name] + k + AHEAD, step * i)
                repeat(act, nq // step, body, peel)

            def run_jobs(js):
                js = list(js)

                def squares(j):
                    J = jobs[j]
                    if J["after"]:
                        act.wait_ge(vector_stage, STAGE[J["after"]])
                    for m, (ap, _, p0, p1) in enumerate(J["srcs"]):
                        n = J["src0"] + m
                        if n >= 4:
                            act.wait_ge(sq_used, n - 3)
                        act.activation(sq[p0:p1, n % 4, 0:J["width"]], ap, ACT.Square).then_inc(sq_ready, 1)

                squares(js[0])
                for i, j in enumerate(js):
                    J = jobs[j]
                    if i + 1 < len(js):
                        squares(js[i + 1])
                    act.wait_ge(stat_ready, j + 1)
                    r = rst[:, j % 2, 0:J["width"]]
                    act.activation(r, r, ACT.Sqrt).then_inc(sqrt_ready, 1)
                    for m, (_, parts, cat, k) in enumerate(J["cat"]):
                        n = J["cat0"] + m
                        act.wait_ge(cat_tmp, n + 1)
                        for a, b, _, shift in parts:
                            if shift is None:
                                last = act.activation(cat[:, k, a:b], tmp[:, n % 2, a:b], ACT.Copy)
                            else:
                                last = act.activation(cat[:, k, a:b], tmp[:, n % 2, a:b], ACT.Identity, bias=shift)
                        last.then_inc(cat_hi, 1)

            def piece(n, nb, cat, k, c0):
                act.wait_ge(piece_ready, n + nb + 1)
                act.activation(pick(cat, k, c0, c0 + S), tmp[:, n % 2, 0:S], ACT.Copy).then_inc(piece_hi, 1)

            def of_tile(func, dst, bank, s, d, no, nb, bias=0.0, width=S):
                act.wait_ge(weights_used, s + d + SLOTS + 1)
                act.wait_ge(sig_used, no + nb + 1)
                act.activation(dst[:, no % 2, 0:width], psum[:, bank, 0:width], func,
                               bias=bias).then_inc(sig_ready, 1)

            act.wait_ge(params_in, 32)
            for n in range(AHEAD):
                hi(n)
            act.wait_ge(x_in, 16)
            run_jobs(JOBS_OF["norm1"])

            def conf(i):
                for k in range(8):
                    s, d = Q0["conf"] + k, 8 * i
                    hi(s + AHEAD, d)
                    if k % 4 == 3:
                        of_tile(ACT.Sigmoid, sig, (T0["conf"] + k // 2) % BANKS, s, d, SIG["conf"] + k // 4, 2 * i)
            repeat(act, 4, conf)

            def sconv(i):
                for k in range(24):
                    s, d = Q0["sconv"] + k, 24 * i
                    hi(s + AHEAD, d)
                    c = k // 6
                    if k % 6 == 1:
                        of_tile(ACT.Copy, sig, (T0["sconv"] + k // 2) % BANKS, s, d, SIG["sconv"] + c, 4 * i)
                    if k % 6 == 5:
                        piece(PIECE["sconv"] + c, 4 * i, hcat, 4 * i + c, S)
            repeat(act, 2, sconv)

            for k in range(16):
                hi(Q0["pool"] + k + AHEAD)
                if k % 2 == 1:
                    piece(PIECE["pooled"] + k // 2, 0, thirdcat, k // 2, 0)
            for k in range(2):
                hi(Q0["mix"] + k + AHEAD)
                for m in range(4):
                    piece(PIECE["mixed"] + 4 * k + m, 0, hcat, KB + 4 * k + m, S)

            def branch(name, r):
                def body(i):
                    for k in range(24):
                        s, d = Q0[name] + k, 24 * i
                        hi(s + AHEAD, d)
                        if k % 3 == 1:
                            t = k // 3
                            of_tile(ACT.Sigmoid, sig, (T0[name] + 2 * t) % BANKS, s, d, SIG[name] + t, 8 * i,
                                    bias=pv("gate_b", 8 * i + (KD * r + t)))
                        if name == "br_b" and k % 3 == 2:
                            piece(PIECE["acc"] + k // 3, 8 * i, hcat, 8 * i + k // 3, S)
                repeat(act, 2, body)

            branch("br_c", 2)
            branch("br_a", 0)
            run_jobs(JOBS_OF["ln"])
            for k in range(KB):
                act.wait_ge(ln_ready, k + 1)
                act.activation(glu[:, k, :], conv[:, k, :], ACT.Sigmoid, bias=pv("ln_b", k)).then_inc(ln_act, 1)
            for k in range(KB):
                act.wait_ge(ln_ready, KB + k + 1)
                act.activation(thirdcat[:, k, 0:S], conv[:, k, :], ACT.Copy).then_inc(ln_act, 1)
            branch("br_b", 1)

            def four_hi(src0, width):
                for k in range(4):
                    act.activation(hcat[:, 4 * k:4 * k + 4, 0:width], X[:, 4 * k:4 * k + 4, src0:src0 + width],
                                   ACT.Copy).then_inc(acc_hi, 1)

            plain("wo", 32, 8)
            run_jobs(JOBS_OF["norm2"])

            def ffn_up(q0, d, n, cb):
                for k in range(4 * n):
                    hi(q0 + k + AHEAD, d)
                    c = k // 4
                    if k % 4 == 1:
                        no = SIG["ffn"] + c
                        act.wait_ge(gate_ready, c + cb + 1)
                        act.wait_ge(sig_used, no + cb + 1)
                        act.activation(sig[:, no % 2, :], half[:, c % 2, :], ACT.Sigmoid).then_inc(sig_ready, 1)
                    if k % 4 == 3:
                        piece(PIECE["ffn"] + c, cb, hcat, c, S)

            def ffn_group(g):
                ffn_up(Q0["ffn"], 48 * g, FF_GROUP, FF_GROUP * g)
                for k in range(16):
                    hi(Q0["ffn"] + 4 * FF_GROUP + k + AHEAD, 48 * g)
            repeat(act, FF_GROUPS, ffn_group)
            ffn_up(Q0["ffn_rest"], 0, FF_REST, FF_GROUPS * FF_GROUP)
            for k in range(16):
                hi(Q0["ffn_rest"] + 4 * FF_REST + k + AHEAD)
            run_jobs(JOBS_OF["final"])

            act.activation(csig[:, :, :].rearrange("p k c -> p (k c)"), pv("cvec", 0, 2 * KD),
                           ACT.Sigmoid).then_inc(c_sig, 1)
            act.wait_ge(c_silu, 1)
            act.activation(ccat[:, :, 0:2], cs[:, :, :], ACT.Copy).then_inc(c_sig, 1)
            plain("ada", 96 * LAYERS, 16)

            def values(name):
                for n in VTS_OF[name]:
                    act.wait_ge(vt_ready, n + 1)
                    act.activation(vtok[:, :, vts[n][1]:vts[n][1] + P],
                                   psum[:, 6 + n % 2, :].rearrange("p (t c) -> p t c", t=4),
                                   ACT.Copy).then_inc(vt_used, 1)

            def attention(name):
                us = UNITS_OF[name]
                for step in range(len(us) + 2):
                    if step < len(us):
                        u = units[us[step]]
                        no = u["no"]
                        cols = u["nk"] + (u["sink"] is not None)
                        act.wait_ge(max_ready, no + 1)
                        if no >= 3:
                            act.wait_ge(t_ready, no - 2)
                        act.activation(probs[:, no % 3, 0:cols], scores[:, no % 2, 0:cols], ACT.Exp,
                                       bias=stat[:, 4 + no % 4:5 + no % 4], scale=u["scale"],
                                       accum_out=stat[:, 8 + no % 4:9 + no % 4]).then_inc(exp_ready, 1)
                    if step >= 2:
                        u = units[us[step - 2]]
                        no = u["no"]
                        act.wait_ge(t_ready, no + 1)
                        if no >= 2:
                            act.wait_ge(o_ready, no - 1)
                        act.activation(probsT[:, no % 2, 0:u["nk"]], psum[:, T_BANK[no % 2], 0:u["nk"]],
                                       ACT.Copy).then_inc(pt_ready, 1)

            for l in range(LAYERS):
                w = chunks_w(l)
                if l == 0:
                    act.wait_ge(ctx_in, 16)
                run_jobs(JOBS_OF[f"h{l}"])

                def z(i):
                    for k in range(8):
                        s, d = Q0[f"z{l}"] + k, 8 * i
                        hi(s + AHEAD, d)
                        if k % 2 == 1:
                            of_tile(ACT.Sigmoid, tmp, (T0[f"z{l}"] + k // 2) % BANKS, s, d, SIG[f"z{l}"] + k // 2,
                                    4 * i, width=w)
                repeat(act, 4, z)
                plain(f"a{l}", 24, 8)
                run_jobs(JOBS_OF[f"a{l}"])
                values(f"a{l}")
                attention(f"a{l}")
                plain(f"b{l}", 20, 20)
                run_jobs(JOBS_OF[f"b{l}"])
                values(f"b{l}")
                attention(f"b{l}")
                plain(f"c{l}", 22, 22)
                run_jobs(JOBS_OF[f"cq{l}"])
                plain(f"qb{l}", 9, 9)
                run_jobs(JOBS_OF[f"ckv{l}"])
                plain(f"kvb{l}", 12, 12)
                run_jobs(JOBS_OF[f"qc{l}"])
                run_jobs(JOBS_OF[f"kc{l}"])
                values(f"c{l}")
                attention(f"c{l}")
                act.wait_ge(vector_stage, STAGE[f"y{l}"])
                four_hi(0, w)
                plain(f"out{l}", 32, 8, peel=1 if l == LAYERS - 1 else 0)

        @block.vector
        def _(vec):
            def fence():
                vec.drain()

            def stage(name):
                vec.drain().then_inc(vector_stage, 1)

            def lo(s, d=0):
                if isinstance(d, int) and s + d >= NQ:
                    return
                slot = s % SLOTS
                vec.wait_ge(hi_ready, s + d + 1)
                vec.tensor_tensor(wlo[:, slot, :], raw[:, slot, :], whi[:, s % HI_SLOTS, :].bitcast(F32),
                                  ALU.subtract).then_inc(lo_ready, 1)

            def tile_done(s, d):
                vec.wait_ge(weights_used, s + d + SLOTS + 1)

            def axpy(dst, src, scalar):
                return vec.scalar_tensor_tensor(dst, src, scalar, dst, ALU.mult, ALU.add)

            def run_jobs(js):
                def cat_lo_part(J, m):
                    ap, parts, cat, k = J["cat"][m]
                    n = J["cat0"] + m
                    vec.wait_ge(cat_hi, n + 1)
                    for a, b, _, shift in parts:
                        dst, h = cat[:, k, 2 * S + a:2 * S + b], cat[:, k, a:b].bitcast(F32)
                        if shift is None:
                            last = vec.tensor_tensor(dst, tmp[:, n % 2, a:b], h, ALU.subtract)
                        else:
                            last = vec.scalar_tensor_tensor(dst, tmp[:, n % 2, a:b], shift, h, ALU.add, ALU.subtract)
                    last.then_inc(cat_lo, 1)

                for j in js:
                    J = jobs[j]
                    w = J["width"]
                    r = rst[:, j % 2, 0:w]
                    vec.wait_ge(sq_used, J["src0"] + len(J["srcs"]))
                    vec.tensor_scalar(r, psum[:, 4 + j % 2, 0:w], 1.0 / J["n"], EPS, ALU.mult,
                                      ALU.add).then_inc(stat_ready, 1)
                    vec.wait_ge(sqrt_ready, j + 1)
                    vec.reciprocal(r, r)
                    fence()
                    for ap, weight, p0, p1 in J["scale"]:
                        if weight is None:
                            vec.tensor_tensor(ap, ap, rst[p0:p1, j % 2, 0:w], ALU.mult)
                        else:
                            vec.scalar_tensor_tensor(ap, ap, weight, rst[p0:p1, j % 2, 0:w], ALU.mult, ALU.mult)
                    for m, (ap, parts, cat, k) in enumerate(J["cat"]):
                        n = J["cat0"] + m
                        if m >= 2:
                            vec.wait_ge(cat_lo, n - 1)
                        for a, b, weight, _ in parts:
                            vec.scalar_tensor_tensor(tmp[:, n % 2, a:b], ap[:, a:b], weight, rst[:, j % 2, a:b],
                                                     ALU.mult, ALU.mult)
                        vec.drain().then_inc(cat_tmp, 1)
                        if m:
                            cat_lo_part(J, m - 1)
                    if J["cat"]:
                        cat_lo_part(J, len(J["cat"]) - 1)

            vec.sem_inc(psum_free, BANKS)
            vec.sem_inc(sig_used, 2)
            vec.wait_ge(params_in, 32)
            for n in range(AHEAD):
                lo(n)
            vec.wait_ge(x_in, 16)
            run_jobs(JOBS_OF["norm1"])

            def conf(i):
                for k in range(8):
                    s, d = Q0["conf"] + k, 8 * i
                    lo(s + AHEAD, d)
                    if k % 4 == 3:
                        no = SIG["conf"] + k // 4
                        vec.wait_ge(sig_ready, no + 2 * i + 1)
                        vec.tensor_tensor(pick(glu, 2 * i + k // 4, 0, S), psum[:, (T0["conf"] + k // 2 - 1) % BANKS, 0:S],
                                          sig[:, no % 2, :], ALU.mult).then_inc(psum_free, 2)
                        vec.drain().then_inc(sig_used, 1)
            repeat(vec, 4, conf)

            def taps(c, first, n):
                for t in range(first, min(first + n, CONF_K)):
                    wt = pv("conf_w", c * CONF_K + (CONF_K - 1 - t))
                    if t == 0:
                        vec.tensor_scalar(pick(conv, c, 0, S), pick(glu, c, 0, S), wt, pv("conf_b", c),
                                          ALU.mult, ALU.add)
                    else:
                        axpy(pick(conv, c, t, S), pick(glu, c, 0, S - t), wt)
                    fence()

            def sconv(i):
                for k in range(24):
                    s, d = Q0["sconv"] + k, 24 * i
                    lo(s + AHEAD, d)
                    c = k // 6
                    bank = (T0["sconv"] + k // 2) % BANKS
                    if k % 6 == 3:
                        no = SIG["sconv"] + c
                        tile_done(s, d)
                        vec.wait_ge(sig_ready, no + 4 * i + 1)
                        vec.tensor_tensor(half[:, 0, :], psum[:, bank, 0:S], sig[:, no % 2, :],
                                          ALU.mult).then_inc(psum_free, 2)
                        vec.drain().then_inc(sig_used, 1)
                        w0 = SCONV_K * (4 * i + c)
                        vec.tensor_scalar(half[:, 1, :], half[:, 0, :], pv("sconv_w", w0 + 2), None, ALU.mult)
                        for lag in (1, 2):
                            fence()
                            axpy(half[:, 1, lag:S], half[:, 0, 0:S - lag], pv("sconv_w", w0 + 2 - lag))
                        fence()
                    if k % 6 == 5:
                        n = PIECE["sconv"] + c
                        tile_done(s, d)
                        vec.wait_ge(piece_lo, n + 4 * i + 1)
                        vec.tensor_tensor(tmp[:, n % 2, 0:S], psum[:, bank, 0:S], half[:, 1, :],
                                          ALU.mult).then_inc(psum_free, 1)
                        vec.drain().then_inc(piece_ready, 1)
            repeat(vec, 2, sconv)

            vec.memset(upad[:, :, 0:PADW], 0.0)
            for k in range(16):
                s = Q0["pool"] + k
                lo(s + AHEAD)
                if k % 2 == 1:
                    t = k // 2
                    n = PIECE["pooled"] + t
                    tile_done(s, 0)
                    vec.tensor_copy(upad[:, 0, PADW:], psum[:, (T0["pool"] + t) % BANKS, 0:S]).then_inc(psum_free, 1)
                    shift, m = 1, 0
                    while shift < POOL_WINDOWS[t // 2]:
                        fence()
                        vec.tensor_tensor(upad[:, m + 1, PADW:], upad[:, m, PADW:], upad[:, m, PADW - shift:PADW + S - shift],
                                          ALU.add)
                        shift, m = 2 * shift, m + 1
                    fence()
                    vec.tensor_scalar(half[:, 0, PADW:], upad[:, m, 2 * PADW:], 1.0 / POOL_WINDOWS[t // 2], None, ALU.mult)
                    vec.tensor_tensor(half[:, 0, 0:PADW], upad[:, m, PADW:2 * PADW],
                                      cv("invcount", PADW * (t // 2), PADW * (t // 2) + PADW), ALU.mult)
                    fence()
                    vec.wait_ge(piece_lo, n + 1)
                    vec.tensor_tensor(tmp[:, n % 2, 0:S], half[:, 0, :], upad[:, 0, PADW:], ALU.subtract)
                    vec.drain().then_inc(piece_ready, 1)
            for k in range(2):
                s = Q0["mix"] + k
                lo(s + AHEAD)
                tile_done(s, 0)
                for m in range(4):
                    t = 4 * k + m
                    n = PIECE["mixed"] + t
                    vec.wait_ge(piece_lo, n + 1)
                    vec.tensor_scalar(tmp[:, n % 2, 0:S], psum[:, (T0["mix"] + t) % BANKS, 0:S], pv("pool_scale", t), None,
                                      ALU.mult).then_inc(psum_free, 1)
                    vec.drain().then_inc(piece_ready, 1)

            def branch(name):
                def body(i):
                    for k in range(24):
                        s, d = Q0[name] + k, 24 * i
                        lo(s + AHEAD, d)
                        if k % 3 == 2:
                            t = k // 3
                            no = SIG[name] + t
                            acc = pick(X, 8 * i + t, S, 2 * S)
                            tile_done(s, d)
                            vec.wait_ge(sig_ready, no + 8 * i + 1)
                            dst = acc if name == "br_c" else half[:, t % 2, :]
                            vec.tensor_tensor(dst, psum[:, (T0[name] + 2 * t + 1) % BANKS, 0:S], sig[:, no % 2, :],
                                              ALU.mult).then_inc(psum_free, 2)
                            vec.drain().then_inc(sig_used, 1)
                            if name == "br_c":
                                taps(POOL_CONV + i, 4 * t, 4)
                            elif name == "br_a":
                                vec.tensor_tensor(acc, acc, dst, ALU.add)
                            else:
                                n = PIECE["acc"] + t
                                vec.wait_ge(piece_lo, n + 8 * i + 1)
                                vec.tensor_tensor(tmp[:, n % 2, 0:S], acc, dst, ALU.add).then_inc(piece_ready, 1)
                repeat(vec, 2, body)

            branch("br_c")
            vec.drain().then_inc(conv_ready, 1)
            branch("br_a")
            vec.wait_ge(mean_ready, 1)
            fence()
            vec.tensor_scalar(half[:, 0, :], psum[:, 6, 0:S], 1.0 / BR, None, ALU.mult)
            fence()
            for k in range(KB):
                vec.tensor_tensor(conv[:, k, :], conv[:, k, :], half[:, 0, :], ALU.subtract)
            stage("centered")
            run_jobs(JOBS_OF["ln"])
            ln_rst = rst[:, JOBS_OF["ln"][0] % 2, 0:S]
            for k in range(KB):
                vec.scalar_tensor_tensor(conv[:, k, :], conv[:, k, :], pv("ln_g", k), ln_rst, ALU.mult,
                                         ALU.mult).then_inc(ln_ready, 1)
            fence()
            for k in range(KB):
                vec.wait_ge(ln_act, k + 1)
                vec.scalar_tensor_tensor(conv[:, k, :], conv[:, k, :], pv("ln_b", k), glu[:, k, :], ALU.add,
                                         ALU.mult).then_inc(ln_ready, 1)
            fence()
            for k in range(KB):
                vec.wait_ge(ln_act, KB + k + 1)
                vec.tensor_tensor(thirdcat[:, k, S:2 * S], conv[:, k, :], thirdcat[:, k, 0:S].bitcast(F32), ALU.subtract)
            stage("third_cat")
            branch("br_b")

            def four_lo(src0, width, first):
                for k in range(4):
                    vec.wait_ge(acc_hi, first + k + 1)
                    c = slice(4 * k, 4 * k + 4)
                    vec.tensor_tensor(hcat[:, c, 2 * S:2 * S + width], X[:, c, src0:src0 + width],
                                      hcat[:, c, 0:width].bitcast(F32), ALU.subtract)

            stage("acc_cat")

            def add_to_x(bank, j):
                xj = pick(X, j, 0, S)
                vec.tensor_tensor(xj, psum[:, bank, 0:S], xj, ALU.add).then_inc(psum_free, 1)

            def wo(i):
                for k in range(8):
                    s, d = Q0["wo"] + k, 8 * i
                    lo(s + AHEAD, d)
                    if k % 2 == 1:
                        tile_done(s, d)
                        add_to_x((T0["wo"] + k // 2) % BANKS, 4 * i + k // 2)
            repeat(vec, 4, wo)
            stage("x_wo")
            vec.wait_ge(piece_lo, PIECE["ffn"] + 2)
            run_jobs(JOBS_OF["norm2"])
            fence()

            def ffn_up(q0, t0, d, n, cb):
                for k in range(4 * n):
                    s = q0 + k
                    lo(s + AHEAD, d)
                    c = k // 4
                    if k % 2 == 1:
                        v = k % 4 // 2
                        u, dst = psum[:, (t0 + k // 2) % BANKS, :], half[:, 2 * v + c % 2, :]
                        w0 = ((cb + c) * 2 + v) * FF_K
                        tile_done(s, d)
                        vec.tensor_scalar(dst, u[:, 0:S], pv("ffn_w", w0 + 2), None, ALU.mult)
                        fence()
                        axpy(dst[:, 1:S], u[:, 0:S - 1], pv("ffn_w", w0 + 1))
                        fence()
                        axpy(dst[:, 2:S], u[:, 0:S - 2], pv("ffn_w", w0)).then_inc(psum_free, 1)
                        if v == 0:
                            vec.drain().then_inc(gate_ready, 1)
                        else:
                            no, m = SIG["ffn"] + c, PIECE["ffn"] + c
                            vec.wait_ge(sig_ready, no + cb + 1)
                            g = half[:, c % 2, :]
                            vec.tensor_tensor(g, g, sig[:, no % 2, :], ALU.mult)
                            vec.drain().then_inc(sig_used, 1)
                            vec.wait_ge(piece_lo, m + cb + 1)
                            vec.tensor_tensor(tmp[:, m % 2, 0:S], g, dst, ALU.mult).then_inc(piece_ready, 1)

            def ffn_down(q0, t0, d):
                for k in range(16):
                    s = q0 + k
                    lo(s + AHEAD, d)
                    tile_done(s, d)
                    add_to_x((t0 + k) % BANKS, k)

            def ffn_group(g):
                ffn_up(Q0["ffn"], T0["ffn"], 48 * g, FF_GROUP, FF_GROUP * g)
                ffn_down(Q0["ffn"] + 4 * FF_GROUP, T0["ffn"] + 2 * FF_GROUP, 48 * g)
            repeat(vec, FF_GROUPS, ffn_group)
            ffn_up(Q0["ffn_rest"], T0["ffn_rest"], 0, FF_REST, FF_GROUPS * FF_GROUP)
            ffn_down(Q0["ffn_rest"] + 4 * FF_REST, T0["ffn_rest"] + 2 * FF_REST, 0)
            stage("x_ffn")
            run_jobs(JOBS_OF["final"])

            vec.wait_ge(c_sig, 1)
            cvec = pv("cvec", 0, 2 * KD).rearrange("p (k c) -> p k c", c=2)
            vec.tensor_tensor(cs[:, :, :], cvec, csig[:, :, :], ALU.mult)
            vec.drain().then_inc(c_silu, 1)
            vec.wait_ge(c_sig, 2)
            vec.tensor_tensor(ccat[:, :, 2:4], cs[:, :, :], ccat[:, :, 0:2].bitcast(F32), ALU.subtract)
            stage("silu_c")

            def ada_blocks(i):
                for k in range(16):
                    lo(Q0["ada"] + k + AHEAD, 16 * i)
                    if k % 8 == 7:
                        b = k // 8
                        tile_done(Q0["ada"] + k, 16 * i)
                        vec.tensor_copy(arow[0:4, b, :], psum[0:4, 4 + b, :])
                        vec.drain().then_inc(rows_ready, 1)
                        vec.wait_ge(fold_ready, 2 * i + b + 1)
                        for c in range(2):
                            vec.tensor_tensor(ada_t[:, c, bass.ds(8 * i + 4 * b, 4)] if not isinstance(i, int) else
                                              ada_t[:, c, 8 * i + 4 * b:8 * i + 4 * b + 4],
                                              psum[:, 6, 8 * b:8 * b + 8].rearrange("p (j c) -> p j c", c=2)[:, :, c],
                                              pv("b_ada", 8 * i + 4 * b, 4), ALU.add)
            repeat(vec, 12, ada_blocks)
            fence()

            def to_chunks(name, nq, q_tile, dst, places, width):
                def one(s, d, bank, j, w):
                    tile_done(s, d)
                    vec.tensor_copy(pick(dst, j, 0, w), psum[:, bank, 0:w]).then_inc(psum_free, 1)
                for k in range(nq):
                    s = Q0[name] + k
                    lo(s + AHEAD)
                    if k % q_tile == q_tile - 1:
                        t = k // q_tile
                        one(s, 0, (T0[name] + t) % BANKS, places[t], width[t])
                stage(name)

            def rope(name):
                for r in ROPES_OF[name]:
                    t = tmp[:, r % 2, 0:S]
                    vec.wait_ge(rot_ready, r + 1)
                    vec.tensor_tensor(t, psum[:, 6 + r % 2, 0:S], cv("sin"), ALU.mult).then_inc(rot_used, 1)
                    vec.tensor_tensor(ropes[r], ropes[r], cv("cos"), ALU.mult)
                    fence()
                    vec.tensor_tensor(ropes[r], ropes[r], t, ALU.add)
                fence()

            def attention(name):
                us = UNITS_OF[name]
                for step in range(len(us) + 4):
                    if step < len(us):
                        u = units[us[step]]
                        no, nk = u["no"], u["nk"]
                        ps, dst = psum[:, 4 + no % 2, :], scores[:, no % 2, :]
                        vec.wait_ge(s_ready, no + 1)
                        if no >= 2:
                            vec.wait_ge(exp_ready, no - 1)
                        a = 0
                        if u["bias"] is not None:
                            b = u["bias"]
                            vec.wait_ge(bias_in[b % 2], 16 * (b // 2 + 1))
                            vec.scalar_tensor_tensor(dst[:, 0:S], bias[:, b % 2, :], 1.0 / u["scale"], ps[:, 0:S],
                                                     ALU.mult, ALU.add)
                            a = S
                        elif "swa" in u:
                            vec.tensor_tensor(dst[:, 0:S], ps[:, 0:S], cv("swa", S * u["swa"], S * u["swa"] + S), ALU.add)
                            a = S
                        vec.tensor_copy(dst[:, a:nk], ps[:, a:nk])
                        if u["sink"] is not None:
                            vec.tensor_scalar(dst[:, nk:nk + 1], u["sink"], 1.0 / u["scale"], None, ALU.mult)
                        fence()
                        cols = nk + (u["sink"] is not None)
                        vec.reduce_max(stat[:, no % 4:no % 4 + 1], dst[:, 0:cols], AX_X)
                        fence()
                        vec.tensor_scalar(stat[:, 4 + no % 4:5 + no % 4], stat[:, no % 4:no % 4 + 1], -u["scale"], None,
                                          ALU.mult).then_inc(max_ready, 1)
                    if 1 <= step <= len(us):
                        no = units[us[step - 1]]["no"]
                        vec.wait_ge(exp_ready, no + 1)
                        vec.reciprocal(stat[:, 12 + no % 4:13 + no % 4],
                                       stat[:, 8 + no % 4:9 + no % 4]).then_inc(rsum_ready, 1)
                    if step >= 4:
                        u = units[us[step - 4]]
                        no, p0, p1 = u["no"], u["p0"], u["p0"] + u["nv"]
                        vec.wait_ge(o_ready, no + 1)
                        y = X[p0:p1, u["y"], u["q0"]:u["q0"] + P]
                        vec.tensor_tensor(y, psum[p0:p1, O_BANK[no % 2], 0:P], y,
                                          ALU.mult).then_inc(o_used, 1)

            def gate_col(c, j):
                return ada_t[:, c, j:j + 1] if isinstance(j, int) else ada_t[:, c, bass.ds(j, 1)]

            for l in range(LAYERS):
                w = chunks_w(l)
                for c in range(2):
                    vec.scalar_tensor_tensor(gain[:, :, c], ada_t[:, c, 48 * l + KD:48 * l + 2 * KD], 1.0,
                                             pv("norm_w", KD * l, KD), ALU.add, ALU.mult)
                stage(f"gains{l}")
                if l == 0:
                    vec.wait_ge(ctx_in, 16)
                    vec.wait_ge(piece_lo, N_PIECES + 2)
                run_jobs(JOBS_OF[f"h{l}"])
                vec.wait_ge(spilled, 16 * (l + 1))

                def z(i):
                    for k in range(8):
                        s, d = Q0[f"z{l}"] + k, 8 * i
                        lo(s + AHEAD, d)
                        if k % 2 == 1:
                            no = SIG[f"z{l}"] + k // 2
                            vec.wait_ge(sig_ready, no + 4 * i + 1)
                            vec.tensor_tensor(pick(X, 4 * i + k // 2, 0, w), psum[:, (T0[f"z{l}"] + k // 2) % BANKS, 0:w],
                                              tmp[:, no % 2, 0:w], ALU.mult).then_inc(psum_free, 1)
                            vec.drain().then_inc(sig_used, 1)
                repeat(vec, 4, z)
                stage(f"z{l}")
                to_chunks(f"a{l}", 24, 2, qkv, range(12), [w] * 4 + [2 * S] * 8)
                run_jobs(JOBS_OF[f"a{l}"])
                stage(f"an{l}")
                attention(f"a{l}")
                to_chunks(f"b{l}", 20, 2, qkv, range(10), [w] * 6 + [2 * S] * 4)
                run_jobs(JOBS_OF[f"b{l}"])
                stage(f"bn{l}")
                rope(f"b{l}")
                stage(f"br{l}")
                attention(f"b{l}")
                to_chunks(f"c{l}", 22, 2, qkv, range(11), [w] * 6 + [2 * S] * 5)
                run_jobs(JOBS_OF[f"cq{l}"])
                to_chunks(f"qb{l}", 9, 1, cqk, range(9), [w] * 9)
                run_jobs(JOBS_OF[f"ckv{l}"])
                to_chunks(f"kvb{l}", 12, 1, cqk, list(range(KN, KN + 6)) + list(range(VC, VC + 6)), [2 * S] * 12)
                run_jobs(JOBS_OF[f"qc{l}"])
                stage(f"qcn{l}")
                rope(f"qc{l}")
                stage(f"qcr{l}")
                vec.tensor_scalar(cqk[:, KR, :], qkv[:, 10, :], pv("kn_cr", l), None, ALU.mult)
                stage(f"kpe{l}")
                rope(f"kpe{l}")
                for t in (1, 2):
                    vec.tensor_copy(cqk[:, KR + t, :], cqk[:, KR, :])
                stage(f"krope{l}")
                run_jobs(JOBS_OF[f"kc{l}"])
                stage(f"kcn{l}")
                attention(f"c{l}")
                stage(f"y{l}")
                four_lo(0, w, 4 * l)
                stage(f"ycat{l}")
                vec.wait_ge(resid_in, 16 * (l + 1))

                def out_tiles(i):
                    for k in range(8):
                        s, d = Q0[f"out{l}"] + k, 8 * i
                        lo(s + AHEAD, d)
                        if k % 2 == 1:
                            j = 4 * i + k // 2
                            bank = (T0[f"out{l}"] + k // 2) % BANKS
                            tile_done(s, d)
                            for c in range(w // S):
                                xj = pick(X, j, S * c, S * c + S)
                                last = vec.scalar_tensor_tensor(xj, psum[:, bank, S * c:S * c + S],
                                                                gate_col(c, 48 * l + 2 * KD + j), xj,
                                                                ALU.mult, ALU.add)
                            last.then_inc(psum_free, 1)
                repeat(vec, 4, out_tiles, peel=1 if l == LAYERS - 1 else 0)
                stage(f"out{l}")

        @block.tensor
        def _(pe):
            def weight(s, col, n=P):
                return whi[:, s % HI_SLOTS, col:col + n], wlo[:, s % SLOTS, col:col + n]

            def tile(s, d, ts, td, cat, c0, loff, width, nq=2, nch=8, k0=0):
                pe.wait_ge(psum_free, ts + td + 1)
                dst = psum[:, ts % BANKS, 0:width]
                for q in range(nq):
                    pe.wait_ge(lo_ready, s + q + d + 1)
                    for k in range(nch):
                        kk = k0 + 8 * q + k
                        h, l_ = weight(s + q, P * k)
                        pe.matmul(dst, h, cat[:, kk, c0:c0 + width], start=(q == 0 and k == 0), stop=False)
                        pe.matmul(dst, h, cat[:, kk, c0 + loff:c0 + loff + width], start=False, stop=False)
                        last = pe.matmul(dst, l_, cat[:, kk, c0:c0 + width], start=False,
                                         stop=(q == nq - 1 and k == nch - 1))
                    last.then_inc(weights_used, 1)

            def tiles(name, count, step, cat, c0, loff, width, peel=0):
                def body(i):
                    for t in range(step):
                        tile(Q0[name] + 2 * t, 2 * step * i, T0[name] + t, step * i, cat, c0, loff, width)
                repeat(pe, count // step, body, peel)

            def run_jobs(js):
                js = list(js)
                for j in js:
                    J = jobs[j]
                    w = J["width"]
                    if j >= 2:
                        pe.wait_ge(stat_ready, j - 1)
                    for m, (_, sel, p0, p1) in enumerate(J["srcs"]):
                        n = J["src0"] + m
                        pe.wait_ge(sq_ready, n + 1)
                        pe.matmul(psum[:, 4 + j % 2, 0:w], sel[p0:p1], sq[p0:p1, n % 4, 0:w], start=(m == 0),
                                  stop=(m == len(J["srcs"]) - 1)).then_inc(sq_used, 1)
                if jobs[js[-1]]["cat"]:
                    J = jobs[js[-1]]
                    pe.wait_ge(cat_lo, J["cat0"] + len(J["cat"]))

            pe.sem_inc(weights_used, SLOTS)
            pe.wait_ge(params_in, 32)
            run_jobs(JOBS_OF["norm1"])
            HC = (hcat, 0, 2 * S, S)
            tiles("conf", 16, 4, *HC)
            tiles("sconv", 24, 12, *HC)
            tiles("pool", 8, 8, *HC)
            pe.wait_ge(piece_lo, PIECE["mixed"] + 2)
            for k in range(2):
                s = Q0["mix"] + k
                pe.wait_ge(lo_ready, s + 1)
                for m in range(4):
                    t = 4 * k + m
                    pe.wait_ge(psum_free, T0["mix"] + t + 1)
                    dst = psum[:, (T0["mix"] + t) % BANKS, 0:S]
                    for c in range(2):
                        h, l_ = weight(s, P * (2 * m + c))
                        src = thirdcat[:, 2 * (t // 2) + c, :]
                        pe.matmul(dst, h, src[:, 0:S], start=(c == 0), stop=False)
                        pe.matmul(dst, h, src[:, S:2 * S], start=False, stop=False)
                        last = pe.matmul(dst, l_, src[:, 0:S], start=False, stop=(c == 1))
                last.then_inc(weights_used, 1)

            def branch(name, cat, c0, loff, k0):
                def body(i):
                    for t in range(8):
                        s, d, ts, td = Q0[name] + 3 * t, 24 * i, T0[name] + 2 * t, 16 * i
                        tile(s, d, ts, td, *HC)
                        tile(s + 2, d, ts + 1, td, cat, c0, loff, S, nq=1, k0=k0)
                repeat(pe, 2, body)

            pe.wait_ge(piece_lo, PIECE["pooled"] + 2)
            branch("br_c", hcat, S, 2 * S, 0)
            pe.wait_ge(piece_lo, PIECE["acc"] + 2)
            branch("br_a", hcat, S, 2 * S, KB)
            pe.wait_ge(conv_ready, 1)
            pe.wait_ge(conv_pool, 1)
            for k in range(KB):
                last = pe.matmul(psum[:, 6, 0:S], ones, conv[:, k, :], start=(k == 0), stop=(k == KB - 1))
            last.then_inc(mean_ready, 1)
            run_jobs(JOBS_OF["ln"])
            pe.wait_ge(vector_stage, STAGE["third_cat"])
            branch("br_b", thirdcat, 0, S, 0)
            pe.wait_ge(piece_lo, PIECE["ffn"] + 2)
            tiles("wo", 16, 4, hcat, S, 2 * S, S)
            run_jobs(JOBS_OF["norm2"])

            def late(q0, d, t0, td, cat, c0, nch, ready, nq=1, early=3):
                held = min(early, HI_SLOTS // nq)
                for first in (True, False):
                    if not first:
                        ready()
                    for t in range(held):
                        if first:
                            pe.wait_ge(psum_free, t0 + t + td + 1)
                        for kk in range(nch - 1) if first else (nch - 1,):
                            q, k = nq * t + kk // 8, kk % 8
                            if first and k == 0:
                                pe.wait_ge(lo_ready, q0 + q + d + 1)
                            h, l_ = weight(q0 + q, P * k)
                            dst = psum[:, (t0 + t) % BANKS, 0:S]
                            pe.matmul(dst, h, cat[:, kk, c0:c0 + S], start=(kk == 0), stop=False)
                            pe.matmul(dst, h, cat[:, kk, c0 + 2 * S:c0 + 3 * S], start=False, stop=False)
                            last = pe.matmul(dst, l_, cat[:, kk, c0:c0 + S], start=False, stop=not first)
                        if not first:
                            last.then_inc(weights_used, nq)
                return held

            def down(q0, d, t0, td, nch, ready):
                for t in range(late(q0, d, t0, td, hcat, S, nch, ready), 16):
                    tile(q0 + t, d, t0 + t, td, hcat, S, 2 * S, S, nq=1, nch=nch)

            def ffn_group(g):
                for t in range(2 * FF_GROUP):
                    tile(Q0["ffn"] + 2 * t, 48 * g, T0["ffn"] + t, 32 * g, *HC)
                pe.wait_ge(piece_lo, FF_GROUP * g + (PIECE["ffn"] + FF_GROUP + 1))
                down(Q0["ffn"] + 4 * FF_GROUP, 48 * g, T0["ffn"] + 2 * FF_GROUP, 32 * g, 8,
                     lambda: pe.wait_ge(piece_lo, FF_GROUP * g + (PIECE["ffn"] + FF_GROUP + 2)))
            repeat(pe, FF_GROUPS, ffn_group)
            for t in range(2 * FF_REST):
                tile(Q0["ffn_rest"] + 2 * t, 0, T0["ffn_rest"] + t, 0, *HC)
            pe.wait_ge(piece_lo, N_PIECES + 1)
            down(Q0["ffn_rest"] + 4 * FF_REST, 0, T0["ffn_rest"] + 2 * FF_REST, 0, FF_REST,
                 lambda: pe.wait_ge(piece_lo, N_PIECES + 2))
            run_jobs(JOBS_OF["final"])
            pe.wait_ge(vector_stage, STAGE["silu_c"])

            def ada_blocks(i):
                for b in range(2):
                    for q in range(8):
                        s = Q0["ada"] + 8 * b + q
                        pe.wait_ge(lo_ready, s + 16 * i + 1)
                        for k in range(2):
                            for m, wt in enumerate(weight(s, 512 * k, 512)):
                                last = pe.matmul(psum[0:4, 4 + b, :], ccat[:, 2 * q + k, :], wt,
                                                 start=(q == 0 and k == 0 and m == 0), stop=(q == 7 and k == 1 and m == 1))
                        last.then_inc(weights_used, 1)
                    pe.wait_ge(rows_ready, 2 * i + b + 1)
                    for j in range(4):
                        last = pe.matmul(psum[:, 6, 8 * b + 2 * j:8 * b + 2 * j + 2], arow[0:4, b, P * j:P * j + P],
                                         cv("fold")[0:4], start=True, stop=True)
                    last.then_inc(fold_ready, 1)
            repeat(pe, 12, ada_blocks)

            def values(name):
                for n in VTS_OF[name]:
                    if n >= 2:
                        pe.wait_ge(vt_used, n - 1)
                    for t in range(4):
                        last = pe.transpose(psum[:, 6 + n % 2, P * t:P * t + P], vts[n][0][:, P * t:P * t + P], cv("ident"))
                    last.then_inc(vt_ready, 1)
                pe.wait_ge(vt_used, VTS_OF[name][-1] + 1)

            def rope(name):
                for r in ROPES_OF[name]:
                    if r >= 2:
                        pe.wait_ge(rot_used, r - 1)
                    pe.matmul(psum[:, 6 + r % 2, 0:S], cv("rot"), ropes[r], start=True, stop=True).then_inc(rot_ready, 1)
                pe.wait_ge(rot_used, ROPES_OF[name][-1] + 1)

            def attention(name):
                us = UNITS_OF[name]
                for step in range(len(us) + 3):
                    if step < len(us):
                        u = units[us[step]]
                        no = u["no"]
                        if no >= 2:
                            pe.wait_ge(max_ready, no - 1)
                        for m, (q, k) in enumerate(u["qk"]):
                            last = pe.matmul(psum[:, 4 + no % 2, 0:u["nk"]], q, k, start=(m == 0),
                                             stop=(m == len(u["qk"]) - 1))
                        last.then_inc(s_ready, 1)
                    if 2 <= step < len(us) + 2:
                        u = units[us[step - 2]]
                        no = u["no"]
                        pe.wait_ge(probs_ready, no + 1)
                        if no >= 2:
                            pe.wait_ge(pt_ready, no - 1)
                        for c in range(u["nk"] // P):
                            last = pe.transpose(psum[:, T_BANK[no % 2], P * c:P * c + P], probs[:, no % 3, P * c:P * c + P], cv("ident"))
                        last.then_inc(t_ready, 1)
                    if step >= 3:
                        u = units[us[step - 3]]
                        no = u["no"]
                        pe.wait_ge(pt_ready, no + 1)
                        if no >= 2:
                            pe.wait_ge(o_used, no - 1)
                        n = u["nk"] // P
                        for c in range(n):
                            last = pe.matmul(psum[u["p0"]:u["p0"] + u["nv"], O_BANK[no % 2], 0:P],
                                             vtok[:, u["k0"] // P + c, u["v"]:u["v"] + u["nv"]],
                                             probsT[:, no % 2, P * c:P * c + P], start=(c == 0), stop=(c == n - 1))
                        last.then_inc(o_ready, 1)
                pe.wait_ge(o_used, us[-1] + 1)

            for l in range(LAYERS):
                w = chunks_w(l)
                run_jobs(JOBS_OF[f"h{l}"])
                tiles(f"z{l}", 16, 4, hcat, 0, 2 * S, w)

                def mixed(name, widths):
                    for t, wt in enumerate(widths):
                        tile(Q0[name] + 2 * t, 0, T0[name] + t, 0, hcat, 0, 2 * S, wt)

                mixed(f"a{l}", [w] * 4 + [2 * S] * 8)
                run_jobs(JOBS_OF[f"a{l}"])
                values(f"a{l}")
                pe.wait_ge(vector_stage, STAGE[f"an{l}"])
                attention(f"a{l}")
                mixed(f"b{l}", [w] * 6 + [2 * S] * 4)
                run_jobs(JOBS_OF[f"b{l}"])
                pe.wait_ge(vector_stage, STAGE[f"bn{l}"])
                rope(f"b{l}")
                values(f"b{l}")
                pe.wait_ge(vector_stage, STAGE[f"br{l}"])
                attention(f"b{l}")
                mixed(f"c{l}", [w] * 6 + [2 * S] * 5)
                run_jobs(JOBS_OF[f"cq{l}"])
                for t in range(9):
                    tile(Q0[f"qb{l}"] + t, 0, T0[f"qb{l}"] + t, 0, hcat, 0, 2 * S, w, nq=1, nch=6, k0=10)
                run_jobs(JOBS_OF[f"ckv{l}"])
                for t in range(12):
                    tile(Q0[f"kvb{l}"] + t, 0, T0[f"kvb{l}"] + t, 0, hcat, 0, 2 * S, 2 * S, nq=1, nch=4, k0=12)
                run_jobs(JOBS_OF[f"qc{l}"])
                pe.wait_ge(vector_stage, STAGE[f"qcn{l}"])
                rope(f"qc{l}")
                pe.wait_ge(vector_stage, STAGE[f"kpe{l}"])
                rope(f"kpe{l}")
                run_jobs(JOBS_OF[f"kc{l}"])
                values(f"c{l}")
                pe.wait_ge(vector_stage, STAGE[f"kcn{l}"])
                attention(f"c{l}")
                pe.wait_ge(vector_stage, STAGE[f"ycat{l}"])
                tiles(f"out{l}", 16, 4, hcat, 0, 2 * S, w)

        @block.gpsimd
        def _(pool):
            def piece(n, nb, cat, k, c0, loff):
                pool.wait_ge(piece_hi, n + nb + 1)
                pool.tensor_tensor(pick(cat, k, c0 + loff, c0 + loff + S), tmp[:, n % 2, 0:S],
                                   pick(cat, k, c0, c0 + S).bitcast(F32), ALU.subtract).then_inc(piece_lo, 1)

            pool.sem_inc(piece_lo, 2)

            def taps(c, first, n):
                for t in range(first, min(first + n, CONF_K)):
                    wt = pv("conf_w", c * CONF_K + (CONF_K - 1 - t))
                    if t == 0:
                        pool.tensor_scalar(pick(conv, c, 0, S), pick(glu, c, 0, S), wt, pv("conf_b", c), ALU.mult,
                                           ALU.add)
                    else:
                        pool.tensor_scalar(tap[:, t % 2, 0:S - t], pick(glu, c, 0, S - t), wt, None, ALU.mult)
                        pool.drain()
                        pool.tensor_tensor(pick(conv, c, t, S), pick(conv, c, t, S), tap[:, t % 2, 0:S - t], ALU.add)
                pool.drain()

            pool.wait_ge(sig_used, SIG["sconv"] + 2)

            for c in range(KB):
                piece(PIECE["sconv"] + c, 0, hcat, c, S, 2 * S)
                taps(c // 4, 8 * (c % 4), 8)
            for t in range(KB):
                piece(PIECE["pooled"] + t, 0, thirdcat, t, 0, S)
            for t in range(KB):
                piece(PIECE["mixed"] + t, 0, hcat, KB + t, S, 2 * S)
            for c in range(2, POOL_CONV):
                taps(c, 0, CONF_K)
            pool.drain().then_inc(conv_pool, 1)
            for t in range(KD):
                piece(PIECE["acc"] + t, 0, hcat, t, S, 2 * S)
            pool.wait_ge(vector_stage, STAGE["acc_cat"])
            pool.dma_start(X[:, :, S:2 * S], ctxT).then_inc(ctx_in, 16)

            def ffn_group(g):
                for c in range(FF_GROUP):
                    piece(PIECE["ffn"] + c, FF_GROUP * g, hcat, c, S, 2 * S)
            repeat(pool, FF_GROUPS, ffn_group)
            for c in range(FF_REST):
                piece(PIECE["ffn"] + c, FF_GROUPS * FF_GROUP, hcat, c, S, 2 * S)

            def load_bias(b):
                l, h, qt = biases[b]
                if b >= 2:
                    prev = next(u for u in units if u["bias"] == b - 2)
                    pool.wait_ge(max_ready, prev["no"] + 1)
                pool.dma_start(bias[:, b % 2, :], natten[l, h, qt]).then_inc(bias_in[b % 2], 16)

            def attention(name):
                us = UNITS_OF[name]
                bs = [units[n]["bias"] for n in us if units[n]["bias"] is not None]
                for b in bs[:2]:
                    load_bias(b)
                for n in us:
                    u = units[n]
                    pool.wait_ge(rsum_ready, n + 1)
                    if u["bias"] is not None and u["bias"] + 2 in bs:
                        load_bias(u["bias"] + 2)
                    p = probs[:, n % 3, 0:u["nk"]]
                    pool.tensor_scalar(p, p, stat[:, 12 + n % 4:13 + n % 4], None, ALU.mult).then_inc(probs_ready, 1)

            for l in range(LAYERS):
                w = chunks_w(l)
                r = resid.rearrange("p (k t) -> p k t", k=KD)[:, :, 0:w]
                pool.wait_ge(ctx_in, 16)
                pool.wait_ge(vector_stage, STAGE[f"gains{l}"])
                pool.dma_start(r, X[:, :, 0:w]).then_inc(spilled, 16)
                pool.wait_ge(vector_stage, STAGE[f"a{l}"])
                attention(f"a{l}")
                attention(f"b{l}")
                attention(f"c{l}")
                pool.wait_ge(vector_stage, STAGE[f"ycat{l}"])
                pool.dma_start(X[:, :, 0:w], r).then_inc(resid_in, 16)
            pool.wait_ge(vector_stage, STAGE[f"out{LAYERS - 1}"])
            pool.dma_start(out, X[:, :, 0:S]).then_inc(out_done, 16)
            pool.wait_ge(out_done, 16)


def _quarters(w):
    k, m = w.shape
    kp = -(-k // (8 * P)) * 8 * P
    if kp != k:
        w = np.concatenate([w, np.zeros((kp - k, m), w.dtype)])
    return w.reshape(kp // (8 * P), 8, P, m // P, P).transpose(3, 0, 2, 1, 4).reshape(m // P, kp // (8 * P), P, QW)


def _stream(w):
    w_in = _quarters(w["w_in"][0])
    parts = []

    def put(a):
        parts.append(a.reshape(-1, P, QW))

    put(w_in[[KB + c + 8 * g for c in range(8) for g in range(2)]])
    put(w_in[[24 + c + o for c in range(8) for o in (8, 16, 0)]])
    put(w_in[0:8])
    put(w["pool_w"][0].reshape(2, 2, 2, P, 2, P).transpose(0, 3, 1, 4, 2, 5))
    for proj, g in (("sconv_proj", 2), ("pool_proj", 0), ("conf_proj", 1)):
        put(np.concatenate([w_in[48 + 16 * g:64 + 16 * g], _quarters(w[proj][0])], axis=1))
    put(_quarters(w["w_o"][0]))
    up = _quarters(w["ffn_up"][0])
    for a in range(0, FF_CH, FF_GROUP):
        b = min(a + FF_GROUP, FF_CH)
        put(up[[c + FF_CH * v for c in range(a, b) for v in range(2)]])
        put(_quarters(w["ffn_down"][0][P * a:P * b]))
    for l in range(LAYERS):
        put(w["w_ada_2"][l].reshape(8, 2, P, 12, 512).transpose(3, 0, 2, 1, 4))
    for l in range(LAYERS):
        u = w["w_in_2"][l]
        qa, ka, va, qb, kb, vb, cq, ckv, kpe, z = np.split(
            u, [512, 1024, 1536, 2304, 2560, 2816, 3584, 4096, 4160], axis=1)
        put(_quarters(np.concatenate([z[:, :512], _heads(z[:, 512:1280], 1), z[:, 1280:]], axis=1)))
        put(_quarters(np.concatenate([qa, ka, va], axis=1)))
        put(_quarters(np.concatenate([_heads(qb, 1), kb, vb], axis=1)))
        put(_quarters(np.concatenate([cq, ckv, kpe, kpe], axis=1)))
        q = w["w_qb_2"][l].reshape(Q_LORA, H_C, QK_C)
        put(_quarters(np.concatenate([q[:, :, :NOPE].reshape(Q_LORA, -1), q[:, :, NOPE:].reshape(Q_LORA, -1)], axis=1)))
        kv = w["w_kvb_2"][l].reshape(KV_LORA, H_C, 2, P)
        put(_quarters(kv.transpose(0, 2, 1, 3).reshape(KV_LORA, -1)))
        o = w["w_out_2"][l]
        put(_quarters(np.concatenate([o[:512], _heads(o[512:1280], 0), o[1280:]], axis=0)))
    return np.concatenate(parts)


def _heads(a, axis):
    a = np.moveaxis(a, axis, 0)
    a = a.reshape(H_B, HD, -1)[B_ORDER].reshape(H_B * HD, -1)
    return np.moveaxis(a, 0, axis)


def _cols(a):
    a = np.asarray(a)
    return a.reshape(-1, P).T


def _params(w):
    twice = lambda a: np.concatenate([a, a], axis=1)
    f = {
        "norm1_g": _cols(w["norm1_g"][0]), "norm2_g": _cols(w["norm2_g"][0]), "final_g": _cols(w["final_g"]),
        "gate_b": _cols(w["gate_b"][0]), "pool_scale": _cols(w["pool_scale"][0]),
        "conf_w": w["conf_conv_w"][0].reshape(CONF_K, KB, P).transpose(2, 1, 0).reshape(P, -1),
        "conf_b": _cols(w["conf_conv_b"][0]), "ln_g": _cols(w["conf_ln_g"][0]), "ln_b": _cols(w["conf_ln_b"][0]),
        "sconv_w": w["sconv_w"][0].reshape(SCONV_K, KB, P).transpose(2, 1, 0).reshape(P, -1),
        "ffn_w": w["ffn_conv_w"][0].reshape(FF_K, 2, FF_CH, P).transpose(3, 2, 1, 0).reshape(P, -1),
        "norm_w": _cols(w["norm_w_2"]), "b_ada": _cols(w["b_ada_2"]),
        "cvec": np.stack([w["c_2"][0].reshape(KD, P), w["c_ctx_2"].reshape(KD, P)]).transpose(2, 1, 0).reshape(P, -1),
        "qn_a": _cols(twice(w["qn_a_2"])), "kn_a": _cols(twice(w["kn_a_2"])),
        "qn_b": _cols(twice(w["qn_b_2"])), "kn_b": _cols(twice(w["kn_b_2"])),
        "qa_norm": _cols(w["qa_norm_2"]), "kva_norm": _cols(w["kva_norm_2"]),
        "qn_cn": _cols(w["qn_c_2"][:, :NOPE]), "qn_cr": _cols(twice(w["qn_c_2"][:, NOPE:])),
        "kn_cn": _cols(w["kn_c_2"][:, :NOPE]), "kn_cr": _cols(twice(w["kn_c_2"][:, NOPE:])),
        "sink": np.broadcast_to(w["sink_b_2"].reshape(1, -1), (P, LAYERS * H_B)),
    }
    return np.ascontiguousarray(np.concatenate([f[n] for n, _ in PARAMS], axis=1))


def _consts():
    ident = np.eye(P)
    ones = np.ones((P, P))
    halves = np.kron(np.eye(2), np.ones((HD, HD)))
    rot = np.zeros((P, P))
    q = HD // 4
    for b in range(0, P, 2 * q):
        for i in range(q):
            rot[b + q + i, b + i] = -1.0
            rot[b + i, b + q + i] = 1.0
    t = np.arange(S)
    inv = np.float32(10000.0) ** (-np.arange(q, dtype=np.float32) / np.float32(q))
    ar = (t // GRID_W).astype(np.float32)[:, None] * inv
    ac = (t % GRID_W).astype(np.float32)[:, None] * inv
    ang = np.concatenate([ar, ar, ac, ac] * 2, axis=1).T.astype(np.float64)
    i = np.arange(S)
    swa = np.where(np.abs(i[:, None] - i[None]) <= SW_WINDOW, 0.0, NEG).reshape(2, P, S).transpose(1, 0, 2)
    f = {"ident": ident, "ones": ones, "halves": halves, "rot": rot, "cos": np.cos(ang), "sin": np.sin(ang),
         "swa": swa.reshape(P, -1), "fold": np.tile(np.eye(2), (P // 2, 1)),
         "invcount": np.broadcast_to(_invcount(), (P, 4 * PADW))}
    return np.concatenate([f[n] for n, _ in CONSTS], axis=1).astype(np.float32)


def _invcount():
    n = np.minimum(np.arange(1, PADW + 1)[None], np.array(POOL_WINDOWS)[:, None])
    return (1.0 / n).reshape(1, -1)


def _natten(rpb):
    t = np.arange(S)
    r, c = t // GRID_W, t % GRID_W
    start = np.clip(c - NA_COLS // 2, 0, GRID_W - NA_COLS)
    ok = (c[None] >= start[:, None]) & (c[None] < start[:, None] + NA_COLS)
    dr = r[None] - r[:, None] + NA_ROWS - 1
    dc = np.clip(c[None] - c[:, None], -(NA_COLS - 1), NA_COLS - 1) + NA_COLS - 1
    placed = rpb[:, :, dr, dc]
    placed[:, :, ~ok] = np.float32(NEG)
    return placed.reshape(LAYERS, H_A, 2, P, S)


def _tokens(a):
    return np.ascontiguousarray(a.reshape(S, KD, P).transpose(2, 1, 0))


def kernel(**inputs):
    import concourse.bacc as bacc
    from concourse.bass_utils import run_bass_kernel_spmd

    w = {k: np.asarray(v) for k, v in inputs.items()}
    arrays = {
        "stream": _stream(w), "xT": _tokens(w["x"][0]), "ctxT": _tokens(w["ctx_2"][0]), "params": _params(w),
        "consts": _consts(), "natten": _natten(w["rpb_a_2"]),
    }
    nc = bacc.Bacc("TRN2", target_bir_lowering=False, num_devices=1)
    args = [nc.dram_tensor(f"in_{n}", a.shape, mybir.dt.from_np(a.dtype), kind="ExternalInput").ap()
            for n, a in arrays.items()]
    out = nc.dram_tensor("out_x", (P, KD, S), F32, kind="ExternalOutput").ap()
    build(nc, *args, out)
    r = run_bass_kernel_spmd(nc, [{f"in_{n}": a for n, a in arrays.items()}], core_ids=[0])
    got = r.results[0]["out_x"]
    return got.transpose(2, 1, 0).reshape(1, S, D)
```

```python
from contextlib import ExitStack

import numpy as np

import concourse.bass as bass
from concourse import mybir

F32 = mybir.dt.float32
F32R = mybir.dt.float32r
ALU = mybir.AluOpType
ACT = mybir.ActivationFunctionType
AX_X = mybir.AxisListType.X

P = 128
D = 2048
S = 256
KD = D // P
EPS = 1e-6
SLOTS = 8
HI_SLOTS = 4
QW = 8 * P
BANKS = 4
S_BANK = (4, 5, 0, 1)
T_BANK, O_BANK = (6, 2), (7, 3)
BIASES = 4
LATE = 3
AHEAD = 3

BR = 1024
KB = BR // P
POOL_CONV = 6
POOL_WINDOWS = (2, 4, 8, 16)
PADW = 16
CONF_K = 31
SCONV_K = 3
D_FF = 5504
FF_CH = D_FF // P
FF_GROUP = 8
FF_GROUPS = FF_CH // FF_GROUP
FF_REST = FF_CH - FF_GROUPS * FF_GROUP
FF_K = 3

LAYERS = 2
HD = 64
H_A, H_B, HKV_B, H_C = 8, 12, 4, 6
QK_C = 192
NOPE = 128
Q_LORA, KV_LORA = 768, 512
SW_WINDOW = 128
GRID_W = 64
NA_ROWS, NA_COLS = 8, 16
NEG = -1e30

B_ORDER = [3 * (2 * t + a) + i for t in range(2) for i in range(3) for a in range(2)]

ADA_BLOCKS = LAYERS * 3 * D // 512
MOD_FFN = [0, 2] + [1, 1, 2] * 4 + [1, 1] + [0] * LATE + [1] * 12 + [0]
MOD_Z = [0, 4, 4, 0]


def weave(quarters, mods):
    out, pos, a, n = [], 0, 0, len(quarters)
    out = [dict(mods=[], rows=[], fold=[], add=[]) for _ in range(n)]
    for t, (nq, m) in enumerate(zip(quarters, mods)):
        out[t].update(pos=pos, nq=nq)
        pos += nq
        for _ in range(m):
            out[t]["mods"].append((pos, a))
            if a % 8 == 7:
                for lag, what in enumerate(("rows", "fold", "add")):
                    out[min(t + 1 + lag, n - 1)][what].append(a // 8)
            pos, a = pos + 1, a + 1
    assert a % 8 == 0
    return out


FFN_WEAVE = weave([2] * 2 * FF_GROUP + [1] * KD, MOD_FFN)
REST_WEAVE = weave([2] * 2 * FF_REST + [1] * KD, [0] * (2 * FF_REST + KD))
Z_WEAVE = [weave([2] * 4, MOD_Z), weave([2] * 4, [0] * 4)]
FFN_BLOCKS = sum(MOD_FFN) // 8
FFN_Q = 3 * KD + sum(MOD_FFN)
Z_Q = [8 + sum(MOD_Z), 8]
assert FF_GROUPS * FFN_BLOCKS + 4 * sum(MOD_Z) // 8 == ADA_BLOCKS

PHASES = [("conf", 32, 16), ("sconv", 48, 24), ("pool", 16, 8), ("mix", 2, 8),
          ("br_c", 48, 32), ("br_a", 48, 32), ("br_b", 48, 32), ("wo", 32, 16),
          ("ffn", FFN_Q * FF_GROUPS, 32 * FF_GROUPS), ("ffn_rest", 4 * FF_REST + 16, 2 * FF_REST + 16)]
for _l in range(LAYERS):
    PHASES += [(f"z{_l}", 4 * Z_Q[_l], 16), (f"a{_l}", 24, 12), (f"b{_l}", 20, 10), (f"c{_l}", 22, 11),
               (f"kvb{_l}", 12, 12), (f"qb{_l}", 9, 9), (f"out{_l}", 32, 16)]
Q0, T0 = {}, {}
_q = _t = 0
for _name, _nq, _nt in PHASES:
    Q0[_name], T0[_name] = _q, _t
    _q, _t = _q + _nq, _t + _nt
NQ = _q
CHUNKS = {}
for _l in range(LAYERS):
    CHUNKS.update({Q0[f"kvb{_l}"] + _i: KV_LORA // P for _i in range(12)})
    CHUNKS.update({Q0[f"qb{_l}"] + _i: Q_LORA // P for _i in range(9)})
CHUNKS.update({Q0["ffn_rest"] + 4 * FF_REST + _i: FF_REST for _i in range(16)})


def used(s, d):
    return P * CHUNKS.get(s, 8) if isinstance(d, int) and d == 0 else QW


PARAMS = [("norm1_g", KD), ("norm2_g", KD), ("final_g", KD), ("gate_b", 3 * KD), ("pool_scale", KB),
          ("conf_w", KB * CONF_K), ("conf_b", KB), ("ln_g", KB), ("ln_b", KB), ("sconv_w", KB * SCONV_K),
          ("ffn_w", FF_CH * 2 * FF_K), ("norm_w", LAYERS * KD), ("b_ada", LAYERS * 3 * KD), ("cvec", KD * 2),
          ("qn_a", LAYERS), ("kn_a", LAYERS), ("qn_b", LAYERS), ("kn_b", LAYERS),
          ("qa_norm", LAYERS * 6), ("kva_norm", LAYERS * 4), ("qn_cn", LAYERS), ("qn_cr", LAYERS),
          ("kn_cn", LAYERS), ("kn_cr", LAYERS), ("sink", LAYERS * H_B)]
PO = {}
_o = 0
for _name, _n in PARAMS:
    PO[_name] = _o
    _o += _n
NPARAM = _o
CONSTS = [("ident", P), ("ones", P), ("halves", P), ("rot", P), ("cos", S), ("sin", S), ("swa", 2 * P), ("fold", 2), ("invcount", 4 * PADW)]
CO = {}
_o = 0
for _name, _n in CONSTS:
    CO[_name] = _o
    _o += _n
NCONST = _o

STAGES = ["centered", "third_cat", "acc_cat", "silu_c", "x_wo", "x_ffn"]
for _l in range(LAYERS):
    STAGES += [f"{_s}{_l}" for _s in ("gains", "a", "b", "c", "y", "ycat", "out")]
STAGE = {name: n + 1 for n, name in enumerate(STAGES)}


def repeat(eng, count, body, peel=0):
    n = count - peel
    if n > 1:
        with eng.Fori(0, n) as i:
            body(i)
    elif n == 1:
        body(0)
    for i in range(n, count):
        body(i)


def pick(t, j, a, b):
    if isinstance(j, int):
        return t[:, j, a:b]
    return t[:, bass.ds(j, 1), a:b].rearrange("p o c -> p (o c)")


def build(nc, stream, xT, ctxT, params, consts, natten, out):
    resid = nc.dram_tensor("resid_dram", (P, KD * 2 * S), F32, kind="Internal").ap()

    KIB = 1024
    at = {}
    top = [(nc.sbuf_base + 31) // 32 * 32]

    def region(name, size):
        at[name] = top[0]
        top[0] += (size + 31) // 32 * 32
        assert top[0] <= nc.sbuf_usable_end, (name, top[0], nc.sbuf_usable_end)

    def sb(name, shape, dt, where, off=0):
        return nc.alloc_sbuf_tensor_at(name, [P] + list(shape), dt, offset=at[where] + off)

    region("raw", SLOTS * QW * 4)
    region("whi", HI_SLOTS * QW * 4)
    region("x", KD * 2 * S * 4)
    region("hcat", KD * 4 * S * 4)
    region("q", 38 * KIB)
    region("params", NPARAM * 4)
    region("consts", CO["invcount"] * 4)
    region("small", (96 * 2 + KD * 6 + 24 + LAYERS * H_B) * 4)
    region("work", 16 * KIB)
    raw = sb("raw", [SLOTS, QW], F32, "raw")
    wlo = sb("wlo", [SLOTS, QW], F32R, "raw")
    whi = sb("whi", [HI_SLOTS, QW], F32R, "whi")
    X = sb("X", [KD, 2 * S], F32, "x")
    hcat = sb("hcat", [KD, 4 * S], F32R, "hcat")
    thirdcat = sb("thirdcat", [KB, 2 * S], F32R, "q")
    glu = sb("glu", [KB, S], F32, "q", 16 * KIB)
    conv = sb("conv", [KB, S], F32, "q", 24 * KIB)
    qkv = sb("qkv", [12, 2 * S], F32, "q")
    vtok = sb("vtok", [4, 6 * P], F32, "q", 24 * KIB)
    ckvcat = sb("ckvcat", [KV_LORA // P, 4 * S], F32R, "q", 22 * KIB)
    cqk = sb("cqk", [18, 2 * S], F32, "hcat")
    cq_rst = sb("cq_rst", [2 * S], F32, "hcat", 36 * KIB)
    par = sb("par", [NPARAM], F32, "params")
    con = sb("con", [CO["invcount"]], F32, "consts")
    invcount = sb("invcount", [NCONST - CO["invcount"]], F32, "q", 36 * KIB)
    o = 0
    ada_t = sb("ada_t", [2, 96], F32, "small", o); o += 96 * 2 * 4
    gain = sb("gain", [KD, 2], F32, "small", o); o += KD * 2 * 4
    ccat = sb("ccat", [KD, 4], F32R, "small", o); o += KD * 4 * 4
    cs = sb("cs", [KD, 2], F32, "q", 5 * KIB)
    csig = sb("csig", [KD, 2], F32, "q", 6 * KIB)
    stat = sb("stat", [24], F32, "small", o); o += 24 * 4
    sinks = sb("sinks", [LAYERS * H_B], F32, "small", o)
    o = 0
    sq = sb("sq", [4, 2 * S], F32, "work", 0)
    rst = sb("rst", [2, 2 * S], F32, "work", 8 * KIB)
    tmp = sb("tmp", [2, 2 * S], F32, "work", 12 * KIB)
    arow = sb("arow", [2, 512], F32, "q", 0)
    sig = sb("sig", [2, S], F32, "work", 0)
    half = sb("half", [4, S], F32, "work", 2 * KIB)
    tap = sb("tap", [2, S], F32, "q", 32 * KIB)
    upad = sb("upad", [5, PADW + S], F32, "work", 6 * KIB)
    probs = sb("probs", [4, 2 * S], F32, "work", 0)
    probsT = sb("probsT", [3, 4 * P], F32, "work", 8 * KIB)
    bias = sb("bias", [BIASES, S], F32, "q", 16 * KIB)

    def pv(name, i, n=1):
        if isinstance(i, int):
            return par[:, PO[name] + i:PO[name] + i + n]
        return par[:, bass.ds(i + PO[name], n)]

    def cv(name, a=0, b=None):
        n = dict(CONSTS)[name]
        return con[:, CO[name] + a:CO[name] + (n if b is None else b)]

    with ExitStack() as ctx:
        psum = ctx.enter_context(nc.psum_tensor("psum", [P, 8, 512], F32))

        def sem(name):
            return ctx.enter_context(nc.semaphore(name))

        raw_in = [sem(f"raw_in{i}") for i in range(SLOTS)]
        hi_ready = sem("hi_ready")
        lo_ready = sem("lo_ready")
        weights_used = sem("weights_used")
        psum_free = sem("psum_free")
        params_in = sem("params_in")
        x_in = sem("x_in")
        ctx_in = sem("ctx_in")
        vector_stage = sem("vector_stage")
        sq_ready = sem("sq_ready")
        sq_used = sem("sq_used")
        stat_ready = sem("stat_ready")
        sqrt_ready = sem("sqrt_ready")
        cat_tmp = sem("cat_tmp")
        cat_hi = sem("cat_hi")
        cat_lo = sem("cat_lo")
        sig_ready = sem("sig_ready")
        sig_used = sem("sig_used")
        gate_ready = sem("gate_ready")
        piece_ready = sem("piece_ready")
        piece_hi = sem("piece_hi")
        piece_lo = sem("piece_lo")
        conv_pool = sem("conv_pool")
        conv_ready = sem("conv_ready")
        mean_ready = sem("mean_ready")
        ln_ready = sem("ln_ready")
        ln_act = sem("ln_act")
        acc_hi = sem("acc_hi")
        c_sig = sem("c_sig")
        c_silu = sem("c_silu")
        rows_ready = sem("rows_ready")
        fold_ready = sem("fold_ready")
        rope_in = sem("rope_in")
        rot_ready = sem("rot_ready")
        rot_used = sem("rot_used")
        vt_ready = sem("vt_ready")
        vt_used = sem("vt_used")
        s_ready = sem("s_ready")
        max_ready = sem("max_ready")
        exp_ready = sem("exp_ready")
        probs_ready = sem("probs_ready")
        t_ready = sem("t_ready")
        pt_ready = sem("pt_ready")
        o_ready = sem("o_ready")
        o_used = sem("o_used")
        bias_in = [sem(f"bias_in{i}") for i in range(BIASES)]
        spilled = sem("spilled")
        resid_in = sem("resid_in")
        out_done = sem("out_done")

        ones = cv("ones")
        halves = cv("halves")
        jobs = []
        src_no = cat_no = 0

        def job(name, srcs, n, width, scale=(), cat=(), after=None, roped=False):
            nonlocal src_no, cat_no
            jobs.append(dict(name=name, srcs=srcs, n=n, width=width, scale=scale, cat=cat, after=after,
                             roped=roped, no=len(jobs), src0=src_no, cat0=cat_no))
            src_no += len(srcs)
            cat_no += len(cat)

        def whole(ap):
            return (ap, ones, 0, P)

        def xjob(name, gname, goff, after, cat):
            srcs = [whole(X[:, k, 0:S]) for k in range(KD)]
            if cat:
                pieces = [(X[:, k, 0:S], [(0, S, pv(gname, goff + k), None)], hcat, k) for k in range(KD)]
                job(name, srcs, D, S, cat=pieces, after=after)
            else:
                job(name, srcs, D, S, scale=[(X[:, k, 0:S], pv(gname, goff + k), 0, P) for k in range(KD)],
                    after=after)

        JOBS_OF = {}

        def group(name, fill):
            a = len(jobs)
            fill()
            JOBS_OF[name] = range(a, len(jobs))

        def rst_of(j, p0=0, p1=P):
            w = jobs[j]["width"]
            return cq_rst[p0:p1, 0:w] if jobs[j]["name"] == "cq" else rst[p0:p1, j % 2, 0:w]

        group("norm1", lambda: xjob("norm1", "norm1_g", 0, None, True))
        group("ln", lambda: job("ln", [whole(conv[:, k, :]) for k in range(KB)], BR, S, after="centered"))
        group("norm2", lambda: xjob("norm2", "norm2_g", 0, "x_wo", True))
        group("final", lambda: xjob("final", "final_g", 0, "x_ffn", False))

        def chunks_w(l):
            return 2 * S if l == 0 else S

        QROPE, KN, KR = 6, 9, 15

        def layer_jobs(l):
            def hnorm():
                srcs = [whole(X[:, k, :]) for k in range(KD)]
                pieces = [(X[:, k, :], [(0, S, gain[:, k, 0:1], ada_t[:, 0, 48 * l + k:48 * l + k + 1]),
                                        (S, 2 * S, gain[:, k, 1:2], ada_t[:, 1, 48 * l + k:48 * l + k + 1])], hcat, k)
                          for k in range(KD)]
                job(f"h{l}", srcs, D, 2 * S, cat=pieces, after=f"gains{l}")
            group(f"h{l}", hnorm)

            def heads(base, count, pname, width, roped):
                for k in range(count):
                    ap = qkv[:, base + k, 0:width]
                    job(pname, [(ap, halves, 0, P)], HD, width, scale=[(ap, pv(pname, l), 0, P)], roped=roped)

            def ga():
                heads(0, 4, "qn_a", chunks_w(l), False)
                heads(4, 4, "kn_a", 2 * S, False)
            group(f"a{l}", ga)

            def gb():
                heads(0, 6, "qn_b", chunks_w(l), True)
                heads(6, 2, "kn_b", 2 * S, True)
            group(f"b{l}", gb)

            def lora(name, base, count, pname, cat, first):
                w = chunks_w(l) if name == "cq" else 2 * S
                srcs = [whole(qkv[:, base + k, 0:w]) for k in range(count)]
                pieces = [(qkv[:, base + k, 0:w], [(0, w, pv(pname, count * l + k), None)], cat, first + k)
                          for k in range(count)]
                job(name, srcs, P * count, w, cat=pieces)
            group(f"ckv{l}", lambda: lora("ckv", 6, 4, "kva_norm", ckvcat, 0))
            group(f"cq{l}", lambda: lora("cq", 0, 6, "qa_norm", hcat, 10))

            def gq():
                w = chunks_w(l)
                for h in range(H_C):
                    a = HD * (h % 2)
                    rope = cqk[a:a + HD, QROPE + h // 2, 0:w]
                    job("qc", [whole(cqk[:, h, 0:w]), (rope, ones, a, a + HD)], QK_C, w,
                        scale=[(cqk[:, h, 0:w], pv("qn_cn", l), 0, P),
                               (rope, pv("qn_cr", l)[a:a + HD], a, a + HD)], roped=h % 2 == 1)

            def gk():
                for h in range(H_C):
                    a = HD * (h % 2)
                    job("kc", [whole(cqk[:, KN + h, :]), (qkv[a:a + HD, 10, :], ones, a, a + HD)], QK_C, 2 * S,
                        scale=[(cqk[:, KN + h, :], pv("kn_cn", l), 0, P),
                               (cqk[a:a + HD, KR + h // 2, :], None, a, a + HD)])
            group(f"kc{l}", gk)
            group(f"qc{l}", gq)

        for l in range(LAYERS):
            layer_jobs(l)

        ropes, ROPES_OF = [], {}
        for l in range(LAYERS):
            for name, targets in ((f"b{l}", [qkv[:, k, 0:S] for k in range(8)]),
                                  (f"kpe{l}", [cqk[:, KR, 0:S]]),
                                  (f"qc{l}", [cqk[:, QROPE + t, 0:S] for t in range(3)])):
                ROPES_OF[name] = range(len(ropes), len(ropes) + len(targets))
                ropes += targets
        vts, VTS_OF = [], {}
        for l in range(LAYERS):
            for name, src, base, count in ((f"a{l}", qkv, 8, 4), (f"b{l}", qkv, 8, 2), (f"c{l}", qkv, 0, 6)):
                VTS_OF[name] = range(len(vts), len(vts) + count)
                vts += [(src[:, base + k, :], k * P) for k in range(count)]

        def projections(name, l):
            w = chunks_w(l)
            tiles_, items = [], {}

            def at_(u, *item):
                items.setdefault(u, []).append(item)

            def heads_at(js, tile0):
                for n, j in enumerate(js):
                    t = tile0 + n
                    at_(t + 2, "sum", j, 0, 1)
                    at_(t + 2, "fin", j)
                    if jobs[j]["roped"]:
                        at_(t + 3, "rope", ROPES_OF[f"{name}{l}"][n])
                    at_(t + 1, "sq", j, 0, 1, t)

            if name in "ab":
                nt = 12 if name == "a" else 10
                nq_, nv_ = (4, 4) if name == "a" else (6, 2)
                for t in range(nt):
                    tiles_.append((Q0[f"{name}{l}"] + 2 * t, 2, 8, hcat, 0, w if t < nq_ else 2 * S, qkv, t))
                heads_at(JOBS_OF[f"{name}{l}"], 0)
                for n, v in enumerate(VTS_OF[f"{name}{l}"]):
                    at_(nt - nv_ + n + 2, "vt", v, nt - nv_ + n)
            else:
                for t in range(11):
                    tiles_.append((Q0[f"c{l}"] + 2 * t, 2, 8, hcat, 0, 2 * S if t < 5 else w, qkv, t + 6 if t < 5 else t - 5))
                for t in range(12):
                    tiles_.append((Q0[f"kvb{l}"] + t, 1, 4, ckvcat, 0, 2 * S, cqk if t < 6 else qkv, KN + t if t < 6 else t - 6))
                for t in range(9):
                    tiles_.append((Q0[f"qb{l}"] + t, 1, 6, hcat, 10, w, cqk, QROPE + t if t < 3 else t - 3))
                k0, v0, q0_ = 11, 17, 23
                ckv, cq = JOBS_OF[f"ckv{l}"][0], JOBS_OF[f"cq{l}"][0]
                at_(4, "sq", ckv, 0, 4, 3)
                at_(5, "sum", ckv, 0, 4)
                at_(5, "fin", ckv)
                for m in range(5):
                    at_(6 + m, "cat", ckv, m)
                at_(9, "sq", cq, 0, 3, 7)
                at_(10, "sum", cq, 0, 3)
                at_(k0, "sq", cq, 3, 6, 10)
                at_(k0 + 1, "sum", cq, 3, 6)
                at_(k0 + 1, "fin", cq)
                at_(k0 + 1, "kpe")
                at_(k0 + 2, "rope", ROPES_OF[f"kpe{l}"][0])
                for m in range(7):
                    at_(k0 + 3 + m, "cat", cq, m)
                for h, j in enumerate(JOBS_OF[f"kc{l}"]):
                    at_(k0 + 3 + h, "sum", j, 0, 2)
                    at_(k0 + 3 + h, "fin", j)
                    at_(k0 + 1 + h, "sq", j, 0, 2, k0 + h)
                for n, v in enumerate(VTS_OF[f"c{l}"]):
                    at_(q0_ + n, "vt", v, v0 + n)
                for h, j in enumerate(JOBS_OF[f"qc{l}"]):
                    t = q0_ + 3 + h
                    at_(t + 2, "sum", j, 0, 2)
                    at_(t + 2, "fin", j)
                    if h % 2:
                        at_(t + 3, "rope", ROPES_OF[f"qc{l}"][h // 2])
                    at_(t + 1, "sq", j, 0, 2, t)
            order = ("sum", "fin", "kpe", "rope", "vt", "cat", "sq")
            for u in items:
                items[u].sort(key=lambda it: order.index(it[0]))
            steps = max(len(tiles_), max(items) + 1)
            return tiles_, [items.get(u, []) for u in range(steps)]

        def copied(first, t):
            return first + t + 1 + BANKS

        units, UNITS_OF = [], {}
        biases = []

        def unit(l, kind, h, qt):
            q0 = P * qt
            ctx_q = qt >= 2
            k0, nk = (S, S) if ctx_q else (0, 2 * S)
            u = dict(no=len(units), kind=kind, nk=nk, k0=k0, q0=q0, bias=None, sink=None)
            if kind == "a":
                a, c = HD * (h % 2), h // 2
                u.update(qk=[(qkv[a:a + HD, c, q0:q0 + P], qkv[a:a + HD, 4 + c, k0:k0 + nk])],
                         v=P * c + a, nv=HD, p0=a, y=c, scale=HD ** -0.5)
                if not ctx_q:
                    u["bias"] = len(biases)
                    biases.append((l, h, qt))
            elif kind == "b":
                c, a = h // 2, HD * (h % 2)
                t = c // 3
                u.update(qk=[(qkv[a:a + HD, c, q0:q0 + P], qkv[a:a + HD, 6 + t, k0:k0 + nk])],
                         v=P * t + a, nv=HD, p0=a, y=4 + c, scale=HD ** -0.5,
                         sink=H_B * l + B_ORDER[h])
                if not ctx_q:
                    u["swa"] = qt
            else:
                a = HD * (h % 2)
                u.update(qk=[(cqk[:, h, q0:q0 + P], cqk[:, KN + h, k0:k0 + nk]),
                             (cqk[a:a + HD, QROPE + h // 2, q0:q0 + P], cqk[a:a + HD, KR + h // 2, k0:k0 + nk])],
                         v=P * h, nv=P, p0=0, y=10 + h, scale=QK_C ** -0.5)
            units.append(u)

        for l in range(LAYERS):
            for kind, heads_ in (("a", H_A), ("b", H_B), ("c", H_C)):
                start = len(units)
                for h in range(heads_):
                    for qt in range(4 if l == 0 else 2):
                        unit(l, kind, h, qt)
                UNITS_OF[f"{kind}{l}"] = range(start, len(units))

        PIECE = {"sconv": 0, "pooled": 8, "mixed": 16, "acc": 24, "ffn": 40}
        N_PIECES = 40 + FF_CH
        SIG = {"conf": 0, "sconv": 8, "br_c": 16, "br_a": 32, "br_b": 48, "ffn": 64, "z0": 64 + FF_CH, "z1": 80 + FF_CH}

        block = ctx.enter_context(nc.Block())

        @block.sync
        def _(sp):
            sp.dma_start(par[:, :], params).then_inc(params_in, 16)
            sp.dma_start(X[:, :, 0:S], xT).then_inc(x_in, 16)
            sp.dma_start(con[:, :], consts[:, 0:CO["invcount"]]).then_inc(params_in, 16)
            sp.dma_start(invcount[:, :], consts[:, CO["invcount"]:]).then_inc(params_in, 16)

            def load(i):
                for k in range(SLOTS):
                    n = SLOTS * i + k
                    sp.wait_ge(weights_used, n + 1)
                    src = stream[n] if isinstance(n, int) else \
                        stream[bass.ds(n, 1)].rearrange("a p c -> p (a c)")
                    sp.dma_start(raw[:, k, :], src).then_inc(raw_in[k], 16)

            repeat(sp, NQ // SLOTS, load)
            for n in range(NQ // SLOTS * SLOTS, NQ):
                sp.wait_ge(weights_used, n + 1)
                sp.dma_start(raw[:, n % SLOTS, :], stream[n]).then_inc(raw_in[n % SLOTS], 16)

        @block.scalar
        def _(act):
            def hi(s, d=0):
                if isinstance(d, int) and s + d >= NQ:
                    return
                slot = s % SLOTS
                act.wait_ge(raw_in[slot], 16 * (s // SLOTS + 1) + 16 // SLOTS * d)
                act.wait_ge(weights_used, s + d + SLOTS - HI_SLOTS + 1)
                c = used(s, d)
                act.activation(whi[:, s % HI_SLOTS, 0:c], raw[:, slot, 0:c], ACT.Copy).then_inc(hi_ready, 1)

            def plain(name, nq, step, peel=0):
                def body(i):
                    for k in range(step):
                        hi(Q0[name] + k + AHEAD, step * i)
                repeat(act, nq // step, body, peel)

            def squares(j, a, b):
                J = jobs[j]
                for m in range(a, b):
                    ap, _, p0, p1 = J["srcs"][m]
                    n = J["src0"] + m
                    if n >= 4:
                        act.wait_ge(sq_used, n - 3)
                    act.activation(sq[p0:p1, n % 4, 0:J["width"]], ap, ACT.Square).then_inc(sq_ready, 1)

            def root(j):
                act.wait_ge(stat_ready, j + 1)
                r = rst_of(j)
                act.activation(r, r, ACT.Sqrt).then_inc(sqrt_ready, 1)

            def cat_hi_part(J, m):
                _, parts, cat, k = J["cat"][m]
                n = J["cat0"] + m
                act.wait_ge(cat_tmp, n + 1)
                for a, b, _, shift in parts:
                    if shift is None:
                        last = act.activation(cat[:, k, a:b], tmp[:, n % 2, a:b], ACT.Copy)
                    else:
                        last = act.activation(cat[:, k, a:b], tmp[:, n % 2, a:b], ACT.Identity, bias=shift)
                last.then_inc(cat_hi, 1)

            def run_job(j):
                J = jobs[j]
                if J["after"]:
                    act.wait_ge(vector_stage, STAGE[J["after"]])
                squares(j, 0, len(J["srcs"]))
                root(j)
                for m in range(len(J["cat"])):
                    cat_hi_part(J, m)

            def piece(n, nb, cat, k, c0):
                act.wait_ge(piece_ready, n + nb + 1)
                act.activation(pick(cat, k, c0, c0 + S), tmp[:, n % 2, 0:S], ACT.Copy).then_inc(piece_hi, 1)

            def of_tile(func, dst, bank, s, d, no, nb, bias=0.0, width=S):
                act.wait_ge(weights_used, s + d + SLOTS + 1)
                act.wait_ge(sig_used, no + nb + 1)
                act.activation(dst[:, no % 2, 0:width], psum[:, bank, 0:width], func,
                               bias=bias).then_inc(sig_ready, 1)

            act.wait_ge(params_in, 48)
            for n in range(AHEAD):
                hi(n)
            act.wait_ge(x_in, 16)
            run_job(JOBS_OF["norm1"][0])

            def conf(i):
                for k in range(8):
                    s, d = Q0["conf"] + k, 8 * i
                    hi(s + AHEAD, d)
                    if k % 4 == 3:
                        of_tile(ACT.Sigmoid, sig, (T0["conf"] + k // 2) % BANKS, s, d, SIG["conf"] + k // 4, 2 * i)
            repeat(act, 4, conf)

            def sconv(i):
                for k in range(24):
                    s, d = Q0["sconv"] + k, 24 * i
                    hi(s + AHEAD, d)
                    c = k // 6
                    if k % 6 == 1:
                        of_tile(ACT.Copy, sig, (T0["sconv"] + k // 2) % BANKS, s, d, SIG["sconv"] + c, 4 * i)
                    if k % 6 == 5:
                        piece(PIECE["sconv"] + c, 4 * i, hcat, 4 * i + c, S)
            repeat(act, 2, sconv)

            for k in range(16):
                hi(Q0["pool"] + k + AHEAD)
                if k % 2 == 1:
                    piece(PIECE["pooled"] + k // 2, 0, thirdcat, k // 2, 0)
            for k in range(2):
                hi(Q0["mix"] + k + AHEAD)
                for m in range(4):
                    piece(PIECE["mixed"] + 4 * k + m, 0, hcat, KB + 4 * k + m, S)

            def branch(name, r):
                def body(i):
                    for k in range(24):
                        s, d = Q0[name] + k, 24 * i
                        hi(s + AHEAD, d)
                        if k % 3 == 1:
                            t = k // 3
                            of_tile(ACT.Sigmoid, sig, (T0[name] + 2 * t) % BANKS, s, d, SIG[name] + t, 8 * i,
                                    bias=pv("gate_b", 8 * i + (KD * r + t)))
                        if name == "br_b" and k and k % 3 == 0:
                            piece(PIECE["acc"] + k // 3 - 1, 8 * i, hcat, 8 * i + k // 3 - 1, S)
                    if name == "br_b":
                        piece(PIECE["acc"] + 7, 8 * i, hcat, 8 * i + 7, S)
                repeat(act, 2, body)

            branch("br_c", 2)
            branch("br_a", 0)
            run_job(JOBS_OF["ln"][0])
            for k in range(KB):
                act.wait_ge(ln_ready, k + 1)
                act.activation(glu[:, k, :], conv[:, k, :], ACT.Sigmoid, bias=pv("ln_b", k)).then_inc(ln_act, 1)
            for k in range(KB):
                act.wait_ge(ln_ready, KB + k + 1)
                act.activation(thirdcat[:, k, 0:S], conv[:, k, :], ACT.Copy).then_inc(ln_act, 1)
            branch("br_b", 1)

            def four_hi(src0, width):
                for k in range(4):
                    act.activation(hcat[:, 4 * k:4 * k + 4, 0:width], X[:, 4 * k:4 * k + 4, src0:src0 + width],
                                   ACT.Copy).then_inc(acc_hi, 1)

            act.activation(csig[:, :, :].rearrange("p k c -> p (k c)"), pv("cvec", 0, 2 * KD),
                           ACT.Sigmoid).then_inc(c_sig, 1)
            act.wait_ge(c_silu, 1)
            act.activation(ccat[:, :, 0:2], cs[:, :, :], ACT.Copy).then_inc(c_sig, 1)
            plain("wo", 32, 8)
            run_job(JOBS_OF["norm2"][0])

            def ffn(weave_, q0, d, n, cb):
                for t, e in enumerate(weave_):
                    hi(q0 + e["pos"] + AHEAD, d)
                    c = (t - 1) // 2
                    if 0 < t <= 2 * n and t % 2 == 1:
                        no = SIG["ffn"] + c
                        act.wait_ge(gate_ready, c + cb + 1)
                        act.wait_ge(sig_used, no + cb + 1)
                        act.activation(sig[:, no % 2, :], half[:, c % 2, :], ACT.Sigmoid).then_inc(sig_ready, 1)
                    elif 0 < t <= 2 * n:
                        piece(PIECE["ffn"] + c, cb, hcat, c, S)
                    if e["nq"] == 2:
                        hi(q0 + e["pos"] + 1 + AHEAD, d)
                    for pos, _ in e["mods"]:
                        hi(q0 + pos + AHEAD, d)
            repeat(act, FF_GROUPS, lambda g: ffn(FFN_WEAVE, Q0["ffn"], FFN_Q * g, FF_GROUP, FF_GROUP * g))
            ffn(REST_WEAVE, Q0["ffn_rest"], 0, FF_REST, FF_GROUPS * FF_GROUP)
            run_job(JOBS_OF["final"][0])

            def projected(name, l):
                tiles_, items = projections(name, l)
                first = T0[f"{name}{l}"]
                for u, todo in enumerate(items):
                    s, nq = tiles_[u][0:2] if u < len(tiles_) else (None, 0)
                    if nq:
                        hi(s + AHEAD)
                    for it in sorted(todo, key=lambda it: it[0] != "sq"):
                        if it[0] == "fin":
                            root(it[1])
                        elif it[0] == "vt":
                            n = it[1]
                            act.wait_ge(vt_ready, n + 1)
                            act.activation(vtok[:, :, vts[n][1]:vts[n][1] + P],
                                           psum[:, 7, :].rearrange("p (t c) -> p t c", t=4),
                                           ACT.Copy).then_inc(vt_used, 1)
                        elif it[0] == "cat" and it[2] < len(jobs[it[1]]["cat"]):
                            cat_hi_part(jobs[it[1]], it[2])
                        elif it[0] == "sq":
                            act.wait_ge(psum_free, copied(first, it[4]))
                            squares(it[1], it[2], it[3])
                    if nq == 2:
                        hi(s + 1 + AHEAD)

            def attention(name):
                us = UNITS_OF[name]
                for step in range(len(us) + 3):
                    if step < len(us):
                        u = units[us[step]]
                        no = u["no"]
                        negmax = stat[:, 4 + no % 4:5 + no % 4]
                        act.wait_ge(max_ready, no + 1)
                        if no >= 4:
                            act.wait_ge(t_ready, no - 3)
                        if u["sink"] is not None:
                            act.activation(stat[:, 16 + no % 4:17 + no % 4], pv("sink", u["sink"]), ACT.Exp, bias=negmax)
                        act.activation(probs[:, no % 4, 0:u["nk"]], psum[:, S_BANK[no % 4], 0:u["nk"]], ACT.Exp,
                                       bias=negmax, scale=u["scale"],
                                       accum_out=stat[:, 8 + no % 4:9 + no % 4]).then_inc(exp_ready, 1)
                    if step >= 3:
                        u = units[us[step - 3]]
                        no = u["no"]
                        act.wait_ge(t_ready, no + 1)
                        if no >= 3:
                            act.wait_ge(o_ready, no - 2)
                        act.activation(probsT[:, no % 3, 0:u["nk"]], psum[:, T_BANK[no % 2], 0:u["nk"]],
                                       ACT.Copy).then_inc(pt_ready, 1)

            for l in range(LAYERS):
                w = chunks_w(l)
                if l == 0:
                    act.wait_ge(ctx_in, 16)
                run_job(JOBS_OF[f"h{l}"][0])

                def z(i):
                    for t, e in enumerate(Z_WEAVE[l]):
                        s, d = Q0[f"z{l}"] + e["pos"], Z_Q[l] * i
                        hi(s + AHEAD, d)
                        hi(s + 1 + AHEAD, d)
                        of_tile(ACT.Sigmoid, tmp, (T0[f"z{l}"] + t) % BANKS, s + 1, d, SIG[f"z{l}"] + t, 4 * i, width=w)
                        for pos, _ in e["mods"]:
                            hi(Q0[f"z{l}"] + pos + AHEAD, d)
                repeat(act, 4, z)
                for name in "abc":
                    projected(name, l)
                    attention(f"{name}{l}")
                act.wait_ge(vector_stage, STAGE[f"y{l}"])
                four_hi(0, w)
                plain(f"out{l}", 32, 8, peel=1 if l == LAYERS - 1 else 0)

        @block.vector
        def _(vec):
            def fence():
                vec.drain()

            def stage(name):
                vec.drain().then_inc(vector_stage, 1)

            def lo(s, d=0):
                if isinstance(d, int) and s + d >= NQ:
                    return
                slot = s % SLOTS
                vec.wait_ge(hi_ready, s + d + 1)
                c = used(s, d)
                vec.tensor_tensor(wlo[:, slot, 0:c], raw[:, slot, 0:c], whi[:, s % HI_SLOTS, 0:c].bitcast(F32),
                                  ALU.subtract).then_inc(lo_ready, 1)

            def tile_done(s, d):
                vec.wait_ge(weights_used, s + d + SLOTS + 1)

            def axpy(dst, src, scalar):
                return vec.scalar_tensor_tensor(dst, src, scalar, dst, ALU.mult, ALU.add)

            def cat_lo_part(J, m):
                ap, parts, cat, k = J["cat"][m]
                n = J["cat0"] + m
                vec.wait_ge(cat_hi, n + 1)
                for a, b, _, shift in parts:
                    dst, h = cat[:, k, 2 * S + a:2 * S + b], cat[:, k, a:b].bitcast(F32)
                    if shift is None:
                        last = vec.tensor_tensor(dst, tmp[:, n % 2, a:b], h, ALU.subtract)
                    else:
                        last = vec.scalar_tensor_tensor(dst, tmp[:, n % 2, a:b], shift, h, ALU.add, ALU.subtract)
                last.then_inc(cat_lo, 1)

            def deviation(j):
                J = jobs[j]
                w = J["width"]
                r = rst_of(j)
                vec.wait_ge(sq_used, J["src0"] + len(J["srcs"]))
                vec.tensor_scalar(r, psum[:, 4 + j % 2, 0:w], 1.0 / J["n"], EPS, ALU.mult,
                                  ALU.add).then_inc(stat_ready, 1)
                vec.wait_ge(sqrt_ready, j + 1)
                vec.reciprocal(r, r)
                fence()
                for ap, weight, p0, p1 in J["scale"]:
                    if weight is None:
                        vec.tensor_tensor(ap, ap, rst_of(j, p0, p1), ALU.mult)
                    else:
                        vec.scalar_tensor_tensor(ap, ap, weight, rst_of(j, p0, p1), ALU.mult, ALU.mult)

            def cat_chunk(j, m):
                J = jobs[j]
                if m < len(J["cat"]):
                    ap, parts, cat, k = J["cat"][m]
                    n = J["cat0"] + m
                    if m >= 2:
                        vec.wait_ge(cat_lo, n - 1)
                    for a, b, weight, _ in parts:
                        vec.scalar_tensor_tensor(tmp[:, n % 2, a:b], ap[:, a:b], weight, rst_of(j)[:, a:b],
                                                 ALU.mult, ALU.mult)
                    vec.drain().then_inc(cat_tmp, 1)
                if m:
                    cat_lo_part(J, m - 1)

            def run_job(j):
                deviation(j)
                if jobs[j]["cat"]:
                    for m in range(len(jobs[j]["cat"]) + 1):
                        cat_chunk(j, m)

            vec.sem_inc(psum_free, BANKS)
            vec.sem_inc(sig_used, 2)
            vec.wait_ge(params_in, 48)
            for n in range(AHEAD):
                lo(n)
            vec.wait_ge(x_in, 16)
            run_job(JOBS_OF["norm1"][0])

            def conf(i):
                for k in range(8):
                    s, d = Q0["conf"] + k, 8 * i
                    lo(s + AHEAD, d)
                    if k % 4 == 3:
                        no = SIG["conf"] + k // 4
                        vec.wait_ge(sig_ready, no + 2 * i + 1)
                        vec.tensor_tensor(pick(glu, 2 * i + k // 4, 0, S), psum[:, (T0["conf"] + k // 2 - 1) % BANKS, 0:S],
                                          sig[:, no % 2, :], ALU.mult).then_inc(psum_free, 2)
                        vec.drain().then_inc(sig_used, 1)
            repeat(vec, 4, conf)

            def taps(c, first, n):
                for t in range(first, min(first + n, CONF_K)):
                    wt = pv("conf_w", c * CONF_K + (CONF_K - 1 - t))
                    if t == 0:
                        vec.tensor_scalar(pick(conv, c, 0, S), pick(glu, c, 0, S), wt, pv("conf_b", c),
                                          ALU.mult, ALU.add)
                    else:
                        axpy(pick(conv, c, t, S), pick(glu, c, 0, S - t), wt)
                    fence()

            def sconv(i):
                for k in range(24):
                    s, d = Q0["sconv"] + k, 24 * i
                    lo(s + AHEAD, d)
                    c = k // 6
                    bank = (T0["sconv"] + k // 2) % BANKS
                    if k % 6 == 3:
                        no = SIG["sconv"] + c
                        tile_done(s, d)
                        vec.wait_ge(sig_ready, no + 4 * i + 1)
                        vec.tensor_tensor(half[:, 0, :], psum[:, bank, 0:S], sig[:, no % 2, :],
                                          ALU.mult).then_inc(psum_free, 2)
                        vec.drain().then_inc(sig_used, 1)
                        w0 = SCONV_K * (4 * i + c)
                        vec.tensor_scalar(half[:, 1, :], half[:, 0, :], pv("sconv_w", w0 + 2), None, ALU.mult)
                        for lag in (1, 2):
                            fence()
                            axpy(half[:, 1, lag:S], half[:, 0, 0:S - lag], pv("sconv_w", w0 + 2 - lag))
                        fence()
                    if k % 6 == 5:
                        n = PIECE["sconv"] + c
                        tile_done(s, d)
                        vec.wait_ge(piece_lo, n + 4 * i + 1)
                        vec.tensor_tensor(tmp[:, n % 2, 0:S], psum[:, bank, 0:S], half[:, 1, :],
                                          ALU.mult).then_inc(psum_free, 1)
                        vec.drain().then_inc(piece_ready, 1)
            repeat(vec, 2, sconv)

            vec.memset(upad[:, :, 0:PADW], 0.0)
            for k in range(16):
                s = Q0["pool"] + k
                lo(s + AHEAD)
                if k % 2 == 1:
                    t = k // 2
                    n = PIECE["pooled"] + t
                    tile_done(s, 0)
                    vec.tensor_copy(upad[:, 0, PADW:], psum[:, (T0["pool"] + t) % BANKS, 0:S]).then_inc(psum_free, 1)
                    shift, m = 1, 0
                    while shift < POOL_WINDOWS[t // 2]:
                        fence()
                        vec.tensor_tensor(upad[:, m + 1, PADW:], upad[:, m, PADW:], upad[:, m, PADW - shift:PADW + S - shift],
                                          ALU.add)
                        shift, m = 2 * shift, m + 1
                    fence()
                    vec.tensor_scalar(half[:, 0, PADW:], upad[:, m, 2 * PADW:], 1.0 / POOL_WINDOWS[t // 2], None, ALU.mult)
                    vec.tensor_tensor(half[:, 0, 0:PADW], upad[:, m, PADW:2 * PADW],
                                      invcount[:, PADW * (t // 2):PADW * (t // 2) + PADW], ALU.mult)
                    fence()
                    vec.wait_ge(piece_lo, n + 1)
                    vec.tensor_tensor(tmp[:, n % 2, 0:S], half[:, 0, :], upad[:, 0, PADW:], ALU.subtract)
                    vec.drain().then_inc(piece_ready, 1)
            for k in range(2):
                s = Q0["mix"] + k
                lo(s + AHEAD)
                tile_done(s, 0)
                for m in range(4):
                    t = 4 * k + m
                    n = PIECE["mixed"] + t
                    vec.wait_ge(piece_lo, n + 1)
                    vec.tensor_scalar(tmp[:, n % 2, 0:S], psum[:, (T0["mix"] + t) % BANKS, 0:S], pv("pool_scale", t), None,
                                      ALU.mult).then_inc(psum_free, 1)
                    vec.drain().then_inc(piece_ready, 1)

            def branch(name):
                def body(i):
                    for k in range(24):
                        s, d = Q0[name] + k, 24 * i
                        lo(s + AHEAD, d)
                        if k % 3 == 2:
                            t = k // 3
                            no = SIG[name] + t
                            acc = pick(X, 8 * i + t, S, 2 * S)
                            tile_done(s, d)
                            vec.wait_ge(sig_ready, no + 8 * i + 1)
                            dst = acc if name == "br_c" else half[:, t % 2, :]
                            vec.tensor_tensor(dst, psum[:, (T0[name] + 2 * t + 1) % BANKS, 0:S], sig[:, no % 2, :],
                                              ALU.mult).then_inc(psum_free, 2)
                            vec.drain().then_inc(sig_used, 1)
                            if name == "br_c":
                                taps(POOL_CONV + i, 4 * t, 4)
                            elif name == "br_a":
                                vec.tensor_tensor(acc, acc, dst, ALU.add)
                            else:
                                n = PIECE["acc"] + t
                                vec.wait_ge(piece_lo, n + 8 * i + 1)
                                vec.tensor_tensor(tmp[:, n % 2, 0:S], acc, dst, ALU.add).then_inc(piece_ready, 1)
                repeat(vec, 2, body)

            branch("br_c")
            vec.drain().then_inc(conv_ready, 1)
            branch("br_a")
            vec.wait_ge(mean_ready, 1)
            fence()
            vec.tensor_scalar(half[:, 0, :], psum[:, 6, 0:S], 1.0 / BR, None, ALU.mult)
            fence()
            for k in range(KB):
                vec.tensor_tensor(conv[:, k, :], conv[:, k, :], half[:, 0, :], ALU.subtract)
            stage("centered")
            run_job(JOBS_OF["ln"][0])
            ln_rst = rst_of(JOBS_OF["ln"][0])
            for k in range(KB):
                vec.scalar_tensor_tensor(conv[:, k, :], conv[:, k, :], pv("ln_g", k), ln_rst, ALU.mult,
                                         ALU.mult).then_inc(ln_ready, 1)
            fence()
            for k in range(KB):
                vec.wait_ge(ln_act, k + 1)
                vec.scalar_tensor_tensor(conv[:, k, :], conv[:, k, :], pv("ln_b", k), glu[:, k, :], ALU.add,
                                         ALU.mult).then_inc(ln_ready, 1)
            fence()
            for k in range(KB):
                vec.wait_ge(ln_act, KB + k + 1)
                vec.tensor_tensor(thirdcat[:, k, S:2 * S], conv[:, k, :], thirdcat[:, k, 0:S].bitcast(F32), ALU.subtract)
            stage("third_cat")
            branch("br_b")

            def four_lo(src0, width, first):
                for k in range(4):
                    vec.wait_ge(acc_hi, first + k + 1)
                    c = slice(4 * k, 4 * k + 4)
                    vec.tensor_tensor(hcat[:, c, 2 * S:2 * S + width], X[:, c, src0:src0 + width],
                                      hcat[:, c, 0:width].bitcast(F32), ALU.subtract)

            stage("acc_cat")

            def add_to_x(bank, j):
                xj = pick(X, j, 0, S)
                vec.tensor_tensor(xj, psum[:, bank, 0:S], xj, ALU.add).then_inc(psum_free, 1)

            vec.wait_ge(c_sig, 1)
            cvec = pv("cvec", 0, 2 * KD).rearrange("p (k c) -> p k c", c=2)
            vec.tensor_tensor(cs[:, :, :], cvec, csig[:, :, :], ALU.mult)
            vec.drain().then_inc(c_silu, 1)
            vec.wait_ge(c_sig, 2)
            vec.tensor_tensor(ccat[:, :, 2:4], cs[:, :, :], ccat[:, :, 0:2].bitcast(F32), ALU.subtract)
            vec.tensor_scalar(sinks[:, :], pv("sink", 0, LAYERS * H_B), HD ** 0.5, None, ALU.mult)
            stage("silu_c")

            def wo(i):
                for k in range(8):
                    s, d = Q0["wo"] + k, 8 * i
                    lo(s + AHEAD, d)
                    if k % 2 == 1:
                        tile_done(s, d)
                        add_to_x((T0["wo"] + k // 2) % BANKS, 4 * i + k // 2)
            repeat(vec, 4, wo)
            stage("x_wo")
            vec.wait_ge(piece_lo, PIECE["ffn"] + 2)
            run_job(JOBS_OF["norm2"][0])
            fence()

            def mod_rows(e, last, d):
                for b in e["rows"]:
                    tile_done(last, d)
                    vec.tensor_copy(arow[0:4, b % 2, :], psum[0:4, 4 + b % 2, :])
                    vec.drain().then_inc(rows_ready, 1)

            def mod_add(e, block0):
                for b in e["add"]:
                    vec.wait_ge(fold_ready, block0 + b + 1)
                    for c in range(2):
                        j = 4 * block0 + 4 * b
                        dst = ada_t[:, c, j:j + 4] if isinstance(j, int) else ada_t[:, c, bass.ds(j, 4)]
                        vec.tensor_tensor(dst, psum[:, 6, 8 * (b % 2):8 * (b % 2) + 8].rearrange("p (j c) -> p j c", c=2)[:, :, c],
                                          pv("b_ada", j, 4), ALU.add)

            def ffn(weave_, q0, t0, d, n, cb, block0):
                for t, e in enumerate(weave_):
                    for k in range(e["nq"]):
                        lo(q0 + e["pos"] + k + AHEAD, d)
                    s = q0 + e["pos"] + e["nq"] - 1
                    tile_done(s, d)
                    if t < 2 * n:
                        c, v = t // 2, t % 2
                        u, dst = psum[:, (t0 + t) % BANKS, :], half[:, 2 * v + c % 2, :]
                        w0 = ((cb + c) * 2 + v) * FF_K
                        vec.tensor_scalar(dst, u[:, 0:S], pv("ffn_w", w0 + 2), None, ALU.mult)
                        fence()
                        axpy(dst[:, 1:S], u[:, 0:S - 1], pv("ffn_w", w0 + 1))
                        fence()
                        axpy(dst[:, 2:S], u[:, 0:S - 2], pv("ffn_w", w0)).then_inc(psum_free, 1)
                        if v == 0:
                            vec.drain().then_inc(gate_ready, 1)
                        else:
                            no, m = SIG["ffn"] + c, PIECE["ffn"] + c
                            vec.wait_ge(sig_ready, no + cb + 1)
                            g = half[:, c % 2, :]
                            vec.tensor_tensor(g, g, sig[:, no % 2, :], ALU.mult)
                            vec.drain().then_inc(sig_used, 1)
                            vec.wait_ge(piece_lo, m + cb + 1)
                            vec.tensor_tensor(tmp[:, m % 2, 0:S], g, dst, ALU.mult).then_inc(piece_ready, 1)
                    else:
                        add_to_x((t0 + t) % BANKS, t - 2 * n)
                    mod_rows(e, s, d)
                    mod_add(e, block0)
                    for pos, _ in e["mods"]:
                        lo(q0 + pos + AHEAD, d)
            repeat(vec, FF_GROUPS, lambda g: ffn(FFN_WEAVE, Q0["ffn"], T0["ffn"], FFN_Q * g, FF_GROUP, FF_GROUP * g,
                                                 FFN_BLOCKS * g))
            ffn(REST_WEAVE, Q0["ffn_rest"], T0["ffn_rest"], 0, FF_REST, FF_GROUPS * FF_GROUP, 0)
            stage("x_ffn")
            run_job(JOBS_OF["final"][0])

            def projected(name, l):
                tiles_, items = projections(name, l)
                for u, todo in enumerate(items):
                    s, nq = tiles_[u][0:2] if u < len(tiles_) else (None, 0)
                    if nq:
                        lo(s + AHEAD)
                    for it in todo:
                        if it[0] == "fin":
                            deviation(it[1])
                            if jobs[it[1]]["roped"]:
                                vec.drain().then_inc(rope_in, 1)
                        elif it[0] == "kpe":
                            vec.tensor_scalar(cqk[:, KR, :], qkv[:, 10, :], pv("kn_cr", l), None, ALU.mult)
                            vec.drain().then_inc(rope_in, 1)
                        elif it[0] == "rope":
                            r = it[1]
                            t = tmp[:, r % 2, 0:S]
                            vec.wait_ge(rot_ready, r + 1)
                            vec.tensor_tensor(t, psum[:, 6, 0:S], cv("sin"), ALU.mult).then_inc(rot_used, 1)
                            vec.tensor_tensor(ropes[r], ropes[r], cv("cos"), ALU.mult)
                            fence()
                            vec.tensor_tensor(ropes[r], ropes[r], t, ALU.add)
                            fence()
                            if r in ROPES_OF[f"kpe{l}"]:
                                for c in (1, 2):
                                    vec.tensor_copy(cqk[:, KR + c, :], cqk[:, KR, :])
                                fence()
                        elif it[0] == "cat":
                            cat_chunk(it[1], it[2])
                    if nq == 2:
                        lo(s + 1 + AHEAD)
                    if nq:
                        w, dst, j = tiles_[u][5:8]
                        tile_done(s + nq - 1, 0)
                        vec.tensor_copy(dst[:, j, 0:w], psum[:, (T0[f"{name}{l}"] + u) % BANKS, 0:w]).then_inc(psum_free, 1)
                stage(f"{name}{l}")

            def attention(name):
                us = UNITS_OF[name]
                for step in range(len(us) + 5):
                    if step < len(us):
                        u = units[us[step]]
                        no, nk = u["no"], u["nk"]
                        ps = psum[:, S_BANK[no % 4], :]
                        top_, negmax = stat[:, no % 4:no % 4 + 1], stat[:, 4 + no % 4:5 + no % 4]
                        vec.wait_ge(s_ready, no + 1)
                        if u["bias"] is not None:
                            b = u["bias"]
                            vec.wait_ge(bias_in[b % BIASES], 16 * (b // BIASES + 1))
                            vec.scalar_tensor_tensor(ps[:, 0:S], bias[:, b % BIASES, :], 1.0 / u["scale"], ps[:, 0:S],
                                                     ALU.mult, ALU.add)
                            fence()
                        elif "swa" in u:
                            a = P * (1 - u["swa"])
                            vec.tensor_tensor(ps[:, a:a + P], ps[:, a:a + P], cv("swa", P * u["swa"], P * u["swa"] + P), ALU.add)
                            fence()
                        vec.reduce_max(top_, ps[:, 0:nk], AX_X)
                        fence()
                        if u["sink"] is None:
                            vec.tensor_scalar(negmax, top_, -u["scale"], None, ALU.mult).then_inc(max_ready, 1)
                        else:
                            vec.tensor_scalar(negmax, top_, sinks[:, u["sink"]:u["sink"] + 1], -u["scale"], ALU.max,
                                              ALU.mult).then_inc(max_ready, 1)
                    if 1 <= step <= len(us):
                        u = units[us[step - 1]]
                        no = u["no"]
                        total = stat[:, 8 + no % 4:9 + no % 4]
                        vec.wait_ge(exp_ready, no + 1)
                        if u["sink"] is not None:
                            vec.tensor_tensor(total, total, stat[:, 16 + no % 4:17 + no % 4], ALU.add)
                            fence()
                        rsum = stat[:, 12 + no % 4:13 + no % 4]
                        vec.reciprocal(rsum, total)
                        fence()
                        p = probs[:, no % 4, 0:u["nk"]]
                        vec.tensor_scalar(p, p, rsum, None, ALU.mult).then_inc(probs_ready, 1)
                    if step >= 5:
                        u = units[us[step - 5]]
                        no, p0, p1 = u["no"], u["p0"], u["p0"] + u["nv"]
                        vec.wait_ge(o_ready, no + 1)
                        y = X[p0:p1, u["y"], u["q0"]:u["q0"] + P]
                        vec.tensor_tensor(y, psum[p0:p1, O_BANK[no % 2], 0:P], y,
                                          ALU.mult).then_inc(o_used, 1)

            def gate_col(c, j):
                return ada_t[:, c, j:j + 1] if isinstance(j, int) else ada_t[:, c, bass.ds(j, 1)]

            for l in range(LAYERS):
                w = chunks_w(l)
                for c in range(2):
                    vec.scalar_tensor_tensor(gain[:, :, c], ada_t[:, c, 48 * l + KD:48 * l + 2 * KD], 1.0,
                                             pv("norm_w", KD * l, KD), ALU.add, ALU.mult)
                stage(f"gains{l}")
                if l == 0:
                    vec.wait_ge(ctx_in, 16)
                    vec.wait_ge(piece_lo, N_PIECES + 2)
                run_job(JOBS_OF[f"h{l}"][0])
                vec.wait_ge(spilled, 16 * (l + 1))

                def z(i):
                    for t, e in enumerate(Z_WEAVE[l]):
                        s, d = Q0[f"z{l}"] + e["pos"], Z_Q[l] * i
                        lo(s + AHEAD, d)
                        lo(s + 1 + AHEAD, d)
                        no = SIG[f"z{l}"] + t
                        vec.wait_ge(sig_ready, no + 4 * i + 1)
                        vec.tensor_tensor(pick(X, 4 * i + t, 0, w), psum[:, (T0[f"z{l}"] + t) % BANKS, 0:w],
                                          tmp[:, no % 2, 0:w], ALU.mult).then_inc(psum_free, 1)
                        vec.drain().then_inc(sig_used, 1)
                        mod_rows(e, s + 1, d)
                        mod_add(e, FF_GROUPS * FFN_BLOCKS + i)
                        for pos, _ in e["mods"]:
                            lo(Q0[f"z{l}"] + pos + AHEAD, d)
                repeat(vec, 4, z)
                fence()
                for name in "abc":
                    projected(name, l)
                    attention(f"{name}{l}")
                stage(f"y{l}")
                four_lo(0, w, 4 * l)
                stage(f"ycat{l}")
                vec.wait_ge(resid_in, 16 * (l + 1))

                def out_tiles(i):
                    for k in range(8):
                        s, d = Q0[f"out{l}"] + k, 8 * i
                        lo(s + AHEAD, d)
                        if k % 2 == 1:
                            j = 4 * i + k // 2
                            bank = (T0[f"out{l}"] + k // 2) % BANKS
                            tile_done(s, d)
                            for c in range(w // S):
                                xj = pick(X, j, S * c, S * c + S)
                                last = vec.scalar_tensor_tensor(xj, psum[:, bank, S * c:S * c + S],
                                                                gate_col(c, 48 * l + 2 * KD + j), xj,
                                                                ALU.mult, ALU.add)
                            last.then_inc(psum_free, 1)
                repeat(vec, 4, out_tiles, peel=1 if l == LAYERS - 1 else 0)
                stage(f"out{l}")

        @block.tensor
        def _(pe):
            def weight(s, col, n=P):
                return whi[:, s % HI_SLOTS, col:col + n], wlo[:, s % SLOTS, col:col + n]

            def tile(s, d, ts, td, cat, c0, loff, width, nq=2, nch=8, k0=0):
                pe.wait_ge(psum_free, ts + td + 1)
                dst = psum[:, ts % BANKS, 0:width]
                for q in range(nq):
                    pe.wait_ge(lo_ready, s + q + d + 1)
                    for k in range(nch):
                        kk = k0 + 8 * q + k
                        h, l_ = weight(s + q, P * k)
                        pe.matmul(dst, h, cat[:, kk, c0:c0 + width], start=(q == 0 and k == 0), stop=False)
                        pe.matmul(dst, h, cat[:, kk, c0 + loff:c0 + loff + width], start=False, stop=False)
                        last = pe.matmul(dst, l_, cat[:, kk, c0:c0 + width], start=False,
                                         stop=(q == nq - 1 and k == nch - 1))
                    last.then_inc(weights_used, 1)

            def tiles(name, count, step, cat, c0, loff, width, skip=0):
                def body(i, t0=0):
                    if name not in ("z0", "z1"):
                        for t in range(t0, step):
                            tile(Q0[name] + 2 * t, 2 * step * i, T0[name] + t, step * i, cat, c0, loff, width)
                        return
                    l = int(name[1])
                    for t, e in enumerate(Z_WEAVE[l]):
                        if t >= t0:
                            tile(Q0[name] + e["pos"], Z_Q[l] * i, T0[name] + t, step * i, cat, c0, loff, width)
                        mod_fold(e, FF_GROUPS * FFN_BLOCKS + i)
                        mod_quarters(e, Q0[name], Z_Q[l] * i)
                if not skip:
                    repeat(pe, count // step, body)
                else:
                    body(0, skip)
                    with pe.Fori(1, count // step) as i:
                        body(i)

            def mod_quarters(e, q0, d):
                for pos, a in e["mods"]:
                    s, q = q0 + pos, a % 8
                    pe.wait_ge(lo_ready, s + d + 1)
                    for k in range(2):
                        for m, wt in enumerate(weight(s, 512 * k, 512)):
                            last = pe.matmul(psum[0:4, 4 + a // 8 % 2, :], ccat[:, 2 * q + k, :], wt,
                                             start=(q == 0 and k == 0 and m == 0), stop=(q == 7 and k == 1 and m == 1))
                    last.then_inc(weights_used, 1)

            def mod_fold(e, block0):
                for b in e["fold"]:
                    pe.wait_ge(rows_ready, block0 + b + 1)
                    for j in range(4):
                        o_ = 8 * (b % 2) + 2 * j
                        last = pe.matmul(psum[:, 6, o_:o_ + 2], arow[0:4, b % 2, P * j:P * j + P], cv("fold")[0:4],
                                         start=True, stop=True)
                    last.then_inc(fold_ready, 1)

            def first_two(name, j, width):
                J = jobs[j]
                s, t = Q0[name], T0[name]
                pe.wait_ge(psum_free, t + 2)

                def one(tile_, kk):
                    h, l_ = weight(s + 2 * tile_ + kk // 8, P * (kk % 8))
                    dst = psum[:, (t + tile_) % BANKS, 0:width]
                    pe.matmul(dst, h, hcat[:, kk, 0:width], start=(kk == 0), stop=False)
                    pe.matmul(dst, h, hcat[:, kk, 2 * S:2 * S + width], start=False, stop=False)
                    return pe.matmul(dst, l_, hcat[:, kk, 0:width], start=False, stop=(kk == KD - 1))

                pe.wait_ge(lo_ready, s + 3)
                for kk in range(KD):
                    pe.wait_ge(cat_lo, J["cat0"] + kk + 1)
                    last = one(0, kk)
                    if kk < 8:
                        one(1, kk)
                last.then_inc(weights_used, 3)
                pe.wait_ge(lo_ready, s + 4)
                for kk in range(8, KD):
                    last = one(1, kk)
                last.then_inc(weights_used, 1)

            def sums(j, a, b):
                J = jobs[j]
                w = J["width"]
                if a == 0 and j >= 2:
                    pe.wait_ge(stat_ready, j - 1)
                for m in range(a, b):
                    _, sel, p0, p1 = J["srcs"][m]
                    n = J["src0"] + m
                    pe.wait_ge(sq_ready, n + 1)
                    pe.matmul(psum[:, 4 + j % 2, 0:w], sel[p0:p1], sq[p0:p1, n % 4, 0:w], start=(m == 0),
                              stop=(m == len(J["srcs"]) - 1)).then_inc(sq_used, 1)

            def run_job(j):
                sums(j, 0, len(jobs[j]["srcs"]))

            def cat_ready(j):
                J = jobs[j]
                pe.wait_ge(cat_lo, J["cat0"] + len(J["cat"]))

            pe.sem_inc(weights_used, SLOTS)
            pe.wait_ge(params_in, 48)
            run_job(JOBS_OF["norm1"][0])
            HC = (hcat, 0, 2 * S, S)
            first_two("conf", JOBS_OF["norm1"][0], S)
            tiles("conf", 16, 4, *HC, skip=2)
            tiles("sconv", 24, 12, *HC)
            tiles("pool", 8, 8, *HC)
            pe.wait_ge(piece_lo, PIECE["mixed"] + 2)
            for k in range(2):
                s = Q0["mix"] + k
                pe.wait_ge(lo_ready, s + 1)
                for m in range(4):
                    t = 4 * k + m
                    pe.wait_ge(psum_free, T0["mix"] + t + 1)
                    dst = psum[:, (T0["mix"] + t) % BANKS, 0:S]
                    for c in range(2):
                        h, l_ = weight(s, P * (2 * m + c))
                        src = thirdcat[:, 2 * (t // 2) + c, :]
                        pe.matmul(dst, h, src[:, 0:S], start=(c == 0), stop=False)
                        pe.matmul(dst, h, src[:, S:2 * S], start=False, stop=False)
                        last = pe.matmul(dst, l_, src[:, 0:S], start=False, stop=(c == 1))
                last.then_inc(weights_used, 1)

            def branch(name, cat, c0, loff, k0):
                def body(i):
                    for t in range(8):
                        s, d, ts, td = Q0[name] + 3 * t, 24 * i, T0[name] + 2 * t, 16 * i
                        tile(s, d, ts, td, *HC)
                        tile(s + 2, d, ts + 1, td, cat, c0, loff, S, nq=1, k0=k0)
                repeat(pe, 2, body)

            pe.wait_ge(piece_lo, PIECE["pooled"] + 2)
            branch("br_c", hcat, S, 2 * S, 0)
            pe.wait_ge(piece_lo, PIECE["acc"] + 2)
            branch("br_a", hcat, S, 2 * S, KB)
            pe.wait_ge(conv_ready, 1)
            pe.wait_ge(conv_pool, 1)
            for k in range(KB):
                last = pe.matmul(psum[:, 6, 0:S], ones, conv[:, k, :], start=(k == 0), stop=(k == KB - 1))
            last.then_inc(mean_ready, 1)
            run_job(JOBS_OF["ln"][0])
            pe.wait_ge(vector_stage, STAGE["third_cat"])
            branch("br_b", thirdcat, 0, S, 0)
            pe.wait_ge(piece_lo, PIECE["ffn"] + 2)
            tiles("wo", 16, 4, hcat, S, 2 * S, S)
            run_job(JOBS_OF["norm2"][0])

            def late(q0, d, t0, td, nch, ready):
                for first in (True, False):
                    if not first:
                        ready()
                    for t in range(LATE):
                        if first:
                            pe.wait_ge(psum_free, t0 + t + td + 1)
                        for kk in range(nch - 1) if first else (nch - 1,):
                            h, l_ = weight(q0 + t, P * kk)
                            if first and kk == 0:
                                pe.wait_ge(lo_ready, q0 + t + d + 1)
                            dst = psum[:, (t0 + t) % BANKS, 0:S]
                            pe.matmul(dst, h, hcat[:, kk, S:2 * S], start=(kk == 0), stop=False)
                            pe.matmul(dst, h, hcat[:, kk, 3 * S:4 * S], start=False, stop=False)
                            last = pe.matmul(dst, l_, hcat[:, kk, S:2 * S], start=False, stop=not first)
                        if not first:
                            last.then_inc(weights_used, 1)

            def ffn(weave_, q0, d, t0, td, n, ready, block0, skip=0):
                for t, e in enumerate(weave_):
                    s = q0 + e["pos"]
                    if skip <= t < 2 * n:
                        tile(s, d, t0 + t, td, *HC)
                    elif t == 2 * n:
                        ready(n - 1)
                        late(s, d, t0 + t, td, n, lambda: ready(n))
                    elif t >= 2 * n + LATE:
                        tile(s, d, t0 + t, td, hcat, S, 2 * S, S, nq=1, nch=n)
                    mod_fold(e, block0)
                    mod_quarters(e, q0, d)

            def ffn_group(g, skip=0):
                ffn(FFN_WEAVE, Q0["ffn"], FFN_Q * g, T0["ffn"], 32 * g, FF_GROUP,
                    lambda k: pe.wait_ge(piece_lo, FF_GROUP * g + (PIECE["ffn"] + k + 2)), FFN_BLOCKS * g, skip)

            pe.wait_ge(vector_stage, STAGE["silu_c"])
            first_two("ffn", JOBS_OF["norm2"][0], S)
            ffn_group(0, 2)
            with pe.Fori(1, FF_GROUPS) as g:
                ffn_group(g)
            ffn(REST_WEAVE, Q0["ffn_rest"], 0, T0["ffn_rest"], 0, FF_REST,
                lambda k: pe.wait_ge(piece_lo, FF_GROUPS * FF_GROUP + PIECE["ffn"] + k + 2), 0)
            run_job(JOBS_OF["final"][0])

            def projected(name, l):
                tiles_, items = projections(name, l)
                first = T0[f"{name}{l}"]
                for u, todo in enumerate(items):
                    for it in todo:
                        if it[0] == "sum":
                            sums(it[1], it[2], it[3])
                        elif it[0] == "rope":
                            r = it[1]
                            pe.wait_ge(rope_in, r + 1)
                            if r:
                                pe.wait_ge(rot_used, r)
                            pe.matmul(psum[:, 6, 0:S], cv("rot"), ropes[r], start=True, stop=True).then_inc(rot_ready, 1)
                        elif it[0] == "vt":
                            n, t = it[1], it[2]
                            pe.wait_ge(psum_free, copied(first, t))
                            if n:
                                pe.wait_ge(vt_used, n)
                            for c in range(4):
                                last = pe.transpose(psum[:, 7, P * c:P * c + P], vts[n][0][:, P * c:P * c + P], cv("ident"))
                            last.then_inc(vt_ready, 1)
                    if u < len(tiles_):
                        s, nq, nch, cat, k0, w = tiles_[u][0:6]
                        if name == "c" and u == 11:
                            cat_ready(JOBS_OF[f"ckv{l}"][0])
                        if name == "c" and u == 23:
                            cat_ready(JOBS_OF[f"cq{l}"][0])
                        tile(s, 0, first + u, 0, cat, 0, 2 * S, w, nq=nq, nch=nch, k0=k0)
                pe.wait_ge(vt_used, VTS_OF[f"{name}{l}"][-1] + 1)
                pe.wait_ge(vector_stage, STAGE[f"{name}{l}"])

            def attention(name):
                us = UNITS_OF[name]
                for step in range(len(us) + 4):
                    if step < len(us):
                        u = units[us[step]]
                        no = u["no"]
                        if no >= 4:
                            pe.wait_ge(exp_ready, no - 3)
                        for m, (q, k) in enumerate(u["qk"]):
                            last = pe.matmul(psum[:, S_BANK[no % 4], 0:u["nk"]], q, k, start=(m == 0),
                                             stop=(m == len(u["qk"]) - 1))
                        last.then_inc(s_ready, 1)
                    if 3 <= step < len(us) + 3:
                        u = units[us[step - 3]]
                        no = u["no"]
                        pe.wait_ge(probs_ready, no + 1)
                        if no >= 2:
                            pe.wait_ge(pt_ready, no - 1)
                        for c in range(u["nk"] // P):
                            last = pe.transpose(psum[:, T_BANK[no % 2], P * c:P * c + P], probs[:, no % 4, P * c:P * c + P], cv("ident"))
                        last.then_inc(t_ready, 1)
                    if step >= 4:
                        u = units[us[step - 4]]
                        no = u["no"]
                        pe.wait_ge(pt_ready, no + 1)
                        if no >= 2:
                            pe.wait_ge(o_used, no - 1)
                        n = u["nk"] // P
                        for c in range(n):
                            last = pe.matmul(psum[u["p0"]:u["p0"] + u["nv"], O_BANK[no % 2], 0:P],
                                             vtok[:, u["k0"] // P + c, u["v"]:u["v"] + u["nv"]],
                                             probsT[:, no % 3, P * c:P * c + P], start=(c == 0), stop=(c == n - 1))
                        last.then_inc(o_ready, 1)
                pe.wait_ge(o_used, us[-1] + 1)

            for l in range(LAYERS):
                w = chunks_w(l)
                run_job(JOBS_OF[f"h{l}"][0])
                first_two(f"z{l}", JOBS_OF[f"h{l}"][0], w)
                tiles(f"z{l}", 16, 4, hcat, 0, 2 * S, w, skip=2)

                for name in "abc":
                    projected(name, l)
                    attention(f"{name}{l}")
                pe.wait_ge(vector_stage, STAGE[f"ycat{l}"])
                tiles(f"out{l}", 16, 4, hcat, 0, 2 * S, w)

        @block.gpsimd
        def _(pool):
            def piece(n, nb, cat, k, c0, loff):
                pool.wait_ge(piece_hi, n + nb + 1)
                pool.tensor_tensor(pick(cat, k, c0 + loff, c0 + loff + S), tmp[:, n % 2, 0:S],
                                   pick(cat, k, c0, c0 + S).bitcast(F32), ALU.subtract).then_inc(piece_lo, 1)

            pool.sem_inc(piece_lo, 2)

            def taps(c, first, n):
                for t in range(first, min(first + n, CONF_K)):
                    wt = pv("conf_w", c * CONF_K + (CONF_K - 1 - t))
                    if t == 0:
                        pool.tensor_scalar(pick(conv, c, 0, S), pick(glu, c, 0, S), wt, pv("conf_b", c), ALU.mult,
                                           ALU.add)
                    else:
                        pool.tensor_scalar(tap[:, t % 2, 0:S - t], pick(glu, c, 0, S - t), wt, None, ALU.mult)
                        pool.drain()
                        pool.tensor_tensor(pick(conv, c, t, S), pick(conv, c, t, S), tap[:, t % 2, 0:S - t], ALU.add)
                pool.drain()

            pool.wait_ge(sig_used, SIG["sconv"] + 2)

            for c in range(KB):
                piece(PIECE["sconv"] + c, 0, hcat, c, S, 2 * S)
                taps(c // 4, 8 * (c % 4), 8)
            for t in range(KB):
                piece(PIECE["pooled"] + t, 0, thirdcat, t, 0, S)
            for t in range(KB):
                piece(PIECE["mixed"] + t, 0, hcat, KB + t, S, 2 * S)
            for c in range(2, POOL_CONV):
                taps(c, 0, CONF_K)
            pool.drain().then_inc(conv_pool, 1)
            for t in range(KD):
                piece(PIECE["acc"] + t, 0, hcat, t, S, 2 * S)
            pool.wait_ge(vector_stage, STAGE["acc_cat"])
            pool.dma_start(X[:, :, S:2 * S], ctxT).then_inc(ctx_in, 16)

            def ffn_group(g):
                for c in range(FF_GROUP):
                    piece(PIECE["ffn"] + c, FF_GROUP * g, hcat, c, S, 2 * S)
            repeat(pool, FF_GROUPS, ffn_group)
            for c in range(FF_REST):
                piece(PIECE["ffn"] + c, FF_GROUPS * FF_GROUP, hcat, c, S, 2 * S)

            def biases_in(name):
                for n in UNITS_OF[name]:
                    b = units[n]["bias"]
                    if b is not None:
                        if b >= BIASES:
                            prev = next(u for u in units if u["bias"] == b - BIASES)
                            pool.wait_ge(max_ready, prev["no"] + 1)
                        l, h, qt = biases[b]
                        pool.dma_start(bias[:, b % BIASES, :], natten[l, h, qt]).then_inc(bias_in[b % BIASES], 16)

            for l in range(LAYERS):
                w = chunks_w(l)
                r = resid.rearrange("p (k t) -> p k t", k=KD)[:, :, 0:w]
                pool.wait_ge(ctx_in, 16)
                pool.wait_ge(vector_stage, STAGE[f"gains{l}"])
                pool.dma_start(r, X[:, :, 0:w]).then_inc(spilled, 16)
                pool.wait_ge(vt_used, VTS_OF[f"a{l}"][-1] + 1)
                biases_in(f"a{l}")
                pool.wait_ge(vector_stage, STAGE[f"ycat{l}"])
                pool.dma_start(X[:, :, 0:w], r).then_inc(resid_in, 16)
            pool.wait_ge(vector_stage, STAGE[f"out{LAYERS - 1}"])
            pool.dma_start(out, X[:, :, 0:S]).then_inc(out_done, 16)
            pool.wait_ge(out_done, 16)


def _quarters(w):
    k, m = w.shape
    kp = -(-k // (8 * P)) * 8 * P
    if kp != k:
        w = np.concatenate([w, np.zeros((kp - k, m), w.dtype)])
    return w.reshape(kp // (8 * P), 8, P, m // P, P).transpose(3, 0, 2, 1, 4).reshape(m // P, kp // (8 * P), P, QW)


def _stream(w):
    w_in = _quarters(w["w_in"][0])
    parts = []

    def put(a):
        parts.append(a.reshape(-1, P, QW))

    put(w_in[[KB + c + 8 * g for c in range(8) for g in range(2)]])
    put(w_in[[24 + c + o for c in range(8) for o in (8, 16, 0)]])
    put(w_in[0:8])
    put(w["pool_w"][0].reshape(2, 2, 2, P, 2, P).transpose(0, 3, 1, 4, 2, 5))
    for proj, g in (("sconv_proj", 2), ("pool_proj", 0), ("conf_proj", 1)):
        put(np.concatenate([w_in[48 + 16 * g:64 + 16 * g], _quarters(w[proj][0])], axis=1))
    put(_quarters(w["w_o"][0]))
    up = _quarters(w["ffn_up"][0])
    ada = w["w_ada_2"].reshape(LAYERS, 8, 2, P, 12, 512).transpose(0, 4, 1, 3, 2, 5).reshape(-1, P, QW)

    def put_woven(weave_, tiles_, mod0):
        for e, t in zip(weave_, tiles_):
            put(t)
            for _, a_ in e["mods"]:
                put(ada[mod0 + a_])

    for g, a in enumerate(range(0, FF_CH, FF_GROUP)):
        b = min(a + FF_GROUP, FF_CH)
        weave_ = FFN_WEAVE if b - a == FF_GROUP else REST_WEAVE
        tiles_ = [up[c + FF_CH * v] for c in range(a, b) for v in range(2)] + list(_quarters(w["ffn_down"][0][P * a:P * b]))
        put_woven(weave_, tiles_, 8 * FFN_BLOCKS * g)
    for l in range(LAYERS):
        u = w["w_in_2"][l]
        qa, ka, va, qb, kb, vb, cq, ckv, kpe, z = np.split(
            u, [512, 1024, 1536, 2304, 2560, 2816, 3584, 4096, 4160], axis=1)
        zq = _quarters(np.concatenate([z[:, :512], _heads(z[:, 512:1280], 1), z[:, 1280:]], axis=1))
        for i in range(4):
            put_woven(Z_WEAVE[l], zq[4 * i:4 * i + 4], 8 * (FF_GROUPS * FFN_BLOCKS + i))
        put(_quarters(np.concatenate([qa, ka, va], axis=1)))
        put(_quarters(np.concatenate([_heads(qb, 1), kb, vb], axis=1)))
        put(_quarters(np.concatenate([ckv, kpe, kpe, cq], axis=1)))
        kv = w["w_kvb_2"][l].reshape(KV_LORA, H_C, 2, P)
        put(_quarters(kv.transpose(0, 2, 1, 3).reshape(KV_LORA, -1)))
        q = w["w_qb_2"][l].reshape(Q_LORA, H_C, QK_C)
        put(_quarters(np.concatenate([q[:, :, NOPE:].reshape(Q_LORA, -1), q[:, :, :NOPE].reshape(Q_LORA, -1)], axis=1)))
        o = w["w_out_2"][l]
        put(_quarters(np.concatenate([o[:512], _heads(o[512:1280], 0), o[1280:]], axis=0)))
    return np.concatenate(parts)


def _heads(a, axis):
    a = np.moveaxis(a, axis, 0)
    a = a.reshape(H_B, HD, -1)[B_ORDER].reshape(H_B * HD, -1)
    return np.moveaxis(a, 0, axis)


def _cols(a):
    a = np.asarray(a)
    return a.reshape(-1, P).T


def _params(w):
    twice = lambda a: np.concatenate([a, a], axis=1)
    f = {
        "norm1_g": _cols(w["norm1_g"][0]), "norm2_g": _cols(w["norm2_g"][0]), "final_g": _cols(w["final_g"]),
        "gate_b": _cols(w["gate_b"][0]), "pool_scale": _cols(w["pool_scale"][0]),
        "conf_w": w["conf_conv_w"][0].reshape(CONF_K, KB, P).transpose(2, 1, 0).reshape(P, -1),
        "conf_b": _cols(w["conf_conv_b"][0]), "ln_g": _cols(w["conf_ln_g"][0]), "ln_b": _cols(w["conf_ln_b"][0]),
        "sconv_w": w["sconv_w"][0].reshape(SCONV_K, KB, P).transpose(2, 1, 0).reshape(P, -1),
        "ffn_w": w["ffn_conv_w"][0].reshape(FF_K, 2, FF_CH, P).transpose(3, 2, 1, 0).reshape(P, -1),
        "norm_w": _cols(w["norm_w_2"]), "b_ada": _cols(w["b_ada_2"]),
        "cvec": np.stack([w["c_2"][0].reshape(KD, P), w["c_ctx_2"].reshape(KD, P)]).transpose(2, 1, 0).reshape(P, -1),
        "qn_a": _cols(twice(w["qn_a_2"])), "kn_a": _cols(twice(w["kn_a_2"])),
        "qn_b": _cols(twice(w["qn_b_2"])), "kn_b": _cols(twice(w["kn_b_2"])),
        "qa_norm": _cols(w["qa_norm_2"]), "kva_norm": _cols(w["kva_norm_2"]),
        "qn_cn": _cols(w["qn_c_2"][:, :NOPE]), "qn_cr": _cols(twice(w["qn_c_2"][:, NOPE:])),
        "kn_cn": _cols(w["kn_c_2"][:, :NOPE]), "kn_cr": _cols(twice(w["kn_c_2"][:, NOPE:])),
        "sink": np.broadcast_to(w["sink_b_2"].reshape(1, -1), (P, LAYERS * H_B)),
    }
    return np.ascontiguousarray(np.concatenate([f[n] for n, _ in PARAMS], axis=1))


def _consts():
    ident = np.eye(P)
    ones = np.ones((P, P))
    halves = np.kron(np.eye(2), np.ones((HD, HD)))
    rot = np.zeros((P, P))
    q = HD // 4
    for b in range(0, P, 2 * q):
        for i in range(q):
            rot[b + q + i, b + i] = -1.0
            rot[b + i, b + q + i] = 1.0
    t = np.arange(S)
    inv = np.float32(10000.0) ** (-np.arange(q, dtype=np.float32) / np.float32(q))
    ar = (t // GRID_W).astype(np.float32)[:, None] * inv
    ac = (t % GRID_W).astype(np.float32)[:, None] * inv
    ang = np.concatenate([ar, ar, ac, ac] * 2, axis=1).T.astype(np.float64)
    i = np.arange(S)
    swa = np.where(np.abs(i[:, None] - i[None]) <= SW_WINDOW, 0.0, NEG)
    assert not swa[:P, :P].any() and not swa[P:, P:].any()
    swa = np.concatenate([swa[:P, P:], swa[P:, :P]], axis=1)
    f = {"ident": ident, "ones": ones, "halves": halves, "rot": rot, "cos": np.cos(ang), "sin": np.sin(ang),
         "swa": swa, "fold": np.tile(np.eye(2), (P // 2, 1)),
         "invcount": np.broadcast_to(_invcount(), (P, 4 * PADW))}
    return np.concatenate([f[n] for n, _ in CONSTS], axis=1).astype(np.float32)


def _invcount():
    n = np.minimum(np.arange(1, PADW + 1)[None], np.array(POOL_WINDOWS)[:, None])
    return (1.0 / n).reshape(1, -1)


def _natten(rpb):
    t = np.arange(S)
    r, c = t // GRID_W, t % GRID_W
    start = np.clip(c - NA_COLS // 2, 0, GRID_W - NA_COLS)
    ok = (c[None] >= start[:, None]) & (c[None] < start[:, None] + NA_COLS)
    dr = r[None] - r[:, None] + NA_ROWS - 1
    dc = np.clip(c[None] - c[:, None], -(NA_COLS - 1), NA_COLS - 1) + NA_COLS - 1
    placed = rpb[:, :, dr, dc]
    placed[:, :, ~ok] = np.float32(NEG)
    return placed.reshape(LAYERS, H_A, 2, P, S)


def _tokens(a):
    return np.ascontiguousarray(a.reshape(S, KD, P).transpose(2, 1, 0))


def kernel(**inputs):
    import concourse.bacc as bacc
    from concourse.bass_utils import run_bass_kernel_spmd

    w = {k: np.asarray(v) for k, v in inputs.items()}
    arrays = {
        "stream": _stream(w), "xT": _tokens(w["x"][0]), "ctxT": _tokens(w["ctx_2"][0]), "params": _params(w),
        "consts": _consts(), "natten": _natten(w["rpb_a_2"]),
    }
    nc = bacc.Bacc("TRN2", target_bir_lowering=False, num_devices=1)
    args = [nc.dram_tensor(f"in_{n}", a.shape, mybir.dt.from_np(a.dtype), kind="ExternalInput").ap()
            for n, a in arrays.items()]
    out = nc.dram_tensor("out_x", (P, KD, S), F32, kind="ExternalOutput").ap()
    build(nc, *args, out)
    r = run_bass_kernel_spmd(nc, [{f"in_{n}": a for n, a in arrays.items()}], core_ids=[0])
    got = r.results[0]["out_x"]
    return got.transpose(2, 1, 0).reshape(1, S, D)
```
